# Optimizing a Trainium2 kernel written in Bass

```python
import jax, jax.numpy as jnp
from jax import lax
import numpy as np

D_MODEL = 1024
BATCH = 1
SEQ = 256
DEPTH = 2

FOX_HEADS = 8
FOX_HEAD_DIM = 64
FOX_W = FOX_HEADS * FOX_HEAD_DIM
FORGET_BIAS_MEAN = 3.0
FORGET_W_SCALE = 0.1
RET_HEADS = 8
RET_QK_DIM = 64
RET_V_DIM = 128
RET_QK_W = RET_HEADS * RET_QK_DIM
RET_V_W = RET_HEADS * RET_V_DIM
RET_CHUNK = 128
MLA_HEADS = 8
MLA_Q_RANK = 384
MLA_KV_RANK = 256
MLA_NOPE_DIM = 64
MLA_ROPE_DIM = 32
MLA_V_DIM = 64
MLA_QK_DIM = MLA_NOPE_DIM + MLA_ROPE_DIM
MLA_V_W = MLA_HEADS * MLA_V_DIM
N_BRANCHES = 3
Q_BLOCK = 128
ROPE_THETA = 10000.0
RMS_EPS = 1e-6
D_FF = 3584
N_EXPERTS = 8
TOP_K = 2
N_DENSE = (DEPTH + 1) // 2
N_MOE = DEPTH // 2
IN_SPLITS = (FOX_W, FOX_W, FOX_W, FOX_HEADS,
             RET_QK_W, RET_QK_W, RET_V_W, RET_V_W,
             MLA_Q_RANK, MLA_KV_RANK, MLA_ROPE_DIM,
             N_BRANCHES * D_MODEL)
D_IN = 3 * FOX_W + FOX_HEADS + 2 * RET_QK_W + 2 * RET_V_W + MLA_Q_RANK + MLA_KV_RANK + MLA_ROPE_DIM + N_BRANCHES * D_MODEL

kernel_name = "hybrid_fox_retnet_mla_moe_block"

def rmsnorm(x, w):
    xf = x.astype(jnp.float32)
    y = xf * lax.rsqrt(jnp.mean(xf * xf, axis=-1, keepdims=True) + RMS_EPS)
    return (y * w.astype(jnp.float32)).astype(x.dtype)

def rope(x):
    S, d = x.shape[1], x.shape[-1]
    pos = jnp.arange(S, dtype=jnp.float32)
    inv_freq = ROPE_THETA ** (-jnp.arange(0, d, 2, dtype=jnp.float32) / d)
    ang = pos[:, None] * inv_freq[None, :]
    cos = jnp.cos(ang)[None, :, None, :]
    sin = jnp.sin(ang)[None, :, None, :]
    xf = x.astype(jnp.float32)
    x1, x2 = xf[..., : d // 2], xf[..., d // 2:]
    out = jnp.concatenate([x1 * cos - x2 * sin, x2 * cos + x1 * sin], axis=-1)
    return out.astype(x.dtype)

def blocked_causal_attention(q, k, v, decay_cum=None):
    B, S, H, dk = q.shape
    dv = v.shape[-1]
    nb = S // Q_BLOCK
    scale = dk ** -0.5
    kpos = jnp.arange(S)
    qb = q.reshape(B, nb, Q_BLOCK, H, dk).transpose(1, 0, 2, 3, 4)
    idx = jnp.arange(nb)
    if decay_cum is not None:
        d_keys = decay_cum.transpose(0, 2, 1)
        d_q = decay_cum.reshape(B, nb, Q_BLOCK, H).transpose(1, 0, 2, 3)
        xs = (idx, qb, d_q)
    else:
        xs = (idx, qb)

    def one_block(args):
        i, qi = args[0], args[1]
        s = jnp.einsum('bqhd,bkhd->bhqk', qi, k).astype(jnp.float32) * scale
        if decay_cum is not None:
            dqi = args[2].transpose(0, 2, 1)
            s = s + (dqi[:, :, :, None] - d_keys[:, :, None, :])
        qpos = i * Q_BLOCK + jnp.arange(Q_BLOCK)
        mask = kpos[None, :] <= qpos[:, None]
        s = jnp.where(mask[None, None], s, -jnp.inf)
        p = jax.nn.softmax(s, axis=-1)
        return jnp.einsum('bhqk,bkhd->bqhd', p.astype(v.dtype), v)

    out = lax.map(one_block, xs)
    return out.transpose(1, 0, 2, 3, 4).reshape(B, S, H, dv)

def retention_chunkwise(q, k, v, gammas):
    B, S, H, dk = q.shape
    dv = v.shape[-1]
    C = RET_CHUNK
    nc = S // C
    qf = q.astype(jnp.float32)
    kf = k.astype(jnp.float32) * (dk ** -0.5)
    vf = v.astype(jnp.float32)
    qc = qf.reshape(B, nc, C, H, dk).transpose(1, 0, 3, 2, 4)
    kc = kf.reshape(B, nc, C, H, dk).transpose(1, 0, 3, 2, 4)
    vc = vf.reshape(B, nc, C, H, dv).transpose(1, 0, 3, 2, 4)
    log_g = jnp.log(gammas)
    j = jnp.arange(C, dtype=jnp.float32)
    diff = j[:, None] - j[None, :]
    d_in = jnp.where(diff[None] >= 0,
                     jnp.exp(jnp.maximum(diff, 0.0)[None] * log_g[:, None, None]), 0.0)
    xi = jnp.exp((j[None, :] + 1.0) * log_g[:, None])
    zeta = jnp.exp((C - 1.0 - j[None, :]) * log_g[:, None])
    g_chunk = jnp.exp(C * log_g)

    def step(R, inp):
        qi, ki, vi = inp
        inner = jnp.einsum('bhnd,bhmd->bhnm', qi, ki) * d_in[None]
        o = jnp.einsum('bhnm,bhme->bhne', inner, vi) \
            + jnp.einsum('bhnd,bhde->bhne', qi, R) * xi[None, :, :, None]
        R = g_chunk[None, :, None, None] * R \
            + jnp.einsum('bhmd,bhme->bhde', ki * zeta[None, :, :, None], vi)
        return R, o

    R0 = jnp.zeros((B, H, dk, dv), jnp.float32)
    _, o = lax.scan(step, R0, (qc, kc, vc))
    return o.transpose(1, 0, 3, 2, 4).reshape(B, S, H, dv)

def hybrid_mixer(h, w_in, fox_f_bias, ret_gn_w, mla_q_norm_w, mla_kv_norm_w,
                 mla_w_uq, mla_w_uk, mla_w_uv, w_br_fox, w_br_ret, w_br_mla, w_out):
    B, S, _ = h.shape
    proj = h @ w_in
    split_at = [int(i) for i in np.cumsum(IN_SPLITS)[:-1]]
    (fq, fk, fv, ff, rq, rk, rv, rg, cq, ckv, kr, gl) = jnp.split(proj, split_at, axis=-1)

    logf = jax.nn.log_sigmoid(ff.astype(jnp.float32) + fox_f_bias.astype(jnp.float32))
    cum = jnp.cumsum(logf, axis=1)
    o_fox = blocked_causal_attention(fq.reshape(B, S, FOX_HEADS, FOX_HEAD_DIM),
                                     fk.reshape(B, S, FOX_HEADS, FOX_HEAD_DIM),
                                     fv.reshape(B, S, FOX_HEADS, FOX_HEAD_DIM),
                                     cum).reshape(B, S, FOX_W)

    r_q = rope(rq.reshape(B, S, RET_HEADS, RET_QK_DIM))
    r_k = rope(rk.reshape(B, S, RET_HEADS, RET_QK_DIM))
    r_v = rv.reshape(B, S, RET_HEADS, RET_V_DIM)
    gammas = 1.0 - 2.0 ** (-5.0 - jnp.arange(RET_HEADS, dtype=jnp.float32))
    o = retention_chunkwise(r_q, r_k, r_v, gammas)
    mu = jnp.mean(o, axis=-1, keepdims=True)
    var = jnp.mean(jnp.square(o - mu), axis=-1, keepdims=True)
    o = (o - mu) * lax.rsqrt(var + RMS_EPS) * ret_gn_w.astype(jnp.float32).reshape(RET_HEADS, RET_V_DIM)
    o_ret = jax.nn.silu(rg) * o.reshape(B, S, RET_V_W).astype(h.dtype)

    c_q = rmsnorm(cq, mla_q_norm_w)
    m_q = (c_q @ mla_w_uq).reshape(B, S, MLA_HEADS, MLA_QK_DIM)
    m_q = jnp.concatenate([m_q[..., :MLA_NOPE_DIM], rope(m_q[..., MLA_NOPE_DIM:])], axis=-1)
    c_kv = rmsnorm(ckv, mla_kv_norm_w)
    k_nope = (c_kv @ mla_w_uk).reshape(B, S, MLA_HEADS, MLA_NOPE_DIM)
    m_v = (c_kv @ mla_w_uv).reshape(B, S, MLA_HEADS, MLA_V_DIM)
    k_rope = rope(kr.reshape(B, S, 1, MLA_ROPE_DIM))
    m_k = jnp.concatenate([k_nope, jnp.broadcast_to(k_rope, (B, S, MLA_HEADS, MLA_ROPE_DIM))], axis=-1)
    o_mla = blocked_causal_attention(m_q, m_k, m_v).reshape(B, S, MLA_V_W)

    gates = jax.nn.sigmoid(gl.reshape(B, S, N_BRANCHES, D_MODEL))
    merged = (gates[:, :, 0] * (o_fox @ w_br_fox)
              + gates[:, :, 1] * (o_ret @ w_br_ret)
              + gates[:, :, 2] * (o_mla @ w_br_mla))
    return merged @ w_out

def swiglu(h, w_gate, w_up, w_down):
    return (jax.nn.silu(h @ w_gate) * (h @ w_up)) @ w_down

def moe_swiglu(h, w_router, w_gate, w_up, w_down):
    logits = (h @ w_router).astype(jnp.float32)
    top_v, top_i = lax.top_k(logits, TOP_K)
    top_w = jax.nn.softmax(top_v, axis=-1)
    combine = jnp.sum(top_w[..., None] * jax.nn.one_hot(top_i, N_EXPERTS, dtype=jnp.float32), axis=-2)
    combine = combine.astype(h.dtype)
    out = jnp.zeros_like(h)
    for e in range(N_EXPERTS):
        out = out + combine[..., e:e + 1] * swiglu(h, w_gate[e], w_up[e], w_down[e])
    return out

def setup_inputs(seed: int = 0) -> dict:
    key = jax.random.key(seed)
    ks = jax.random.split(key, 32)
    f32 = jnp.float32

    def nrm(k, shape, scale):
        return jax.random.normal(k, shape, f32) * scale

    def gain(k, shape):
        return 1.0 + 0.05 * jax.random.normal(k, shape, f32)

    col_scale = jnp.ones((D_IN,), f32).at[3 * FOX_W:3 * FOX_W + FOX_HEADS].set(FORGET_W_SCALE)
    return {
        "x": jax.random.normal(ks[0], (BATCH, SEQ, D_MODEL), f32),
        "norm_mix_w": gain(ks[1], (DEPTH, D_MODEL)),
        "w_in": nrm(ks[2], (DEPTH, D_MODEL, D_IN), D_MODEL ** -0.5) * col_scale,
        "fox_f_bias": FORGET_BIAS_MEAN + 0.5 * jax.random.normal(ks[3], (DEPTH, FOX_HEADS), f32),
        "ret_gn_w": gain(ks[4], (DEPTH, RET_V_W)),
        "mla_q_norm_w": gain(ks[5], (DEPTH, MLA_Q_RANK)),
        "mla_kv_norm_w": gain(ks[6], (DEPTH, MLA_KV_RANK)),
        "mla_w_uq": nrm(ks[7], (DEPTH, MLA_Q_RANK, MLA_HEADS * MLA_QK_DIM), MLA_Q_RANK ** -0.5),
        "mla_w_uk": nrm(ks[8], (DEPTH, MLA_KV_RANK, MLA_HEADS * MLA_NOPE_DIM), MLA_KV_RANK ** -0.5),
        "mla_w_uv": nrm(ks[9], (DEPTH, MLA_KV_RANK, MLA_V_W), MLA_KV_RANK ** -0.5),
        "w_br_fox": nrm(ks[10], (DEPTH, FOX_W, D_MODEL), FOX_W ** -0.5),
        "w_br_ret": nrm(ks[11], (DEPTH, RET_V_W, D_MODEL), RET_V_W ** -0.5),
        "w_br_mla": nrm(ks[12], (DEPTH, MLA_V_W, D_MODEL), MLA_V_W ** -0.5),
        "w_out": nrm(ks[13], (DEPTH, D_MODEL, D_MODEL), D_MODEL ** -0.5),
        "norm_ffn_w": gain(ks[14], (DEPTH, D_MODEL)),
        "dense_w_gate": nrm(ks[15], (N_DENSE, D_MODEL, D_FF), D_MODEL ** -0.5),
        "dense_w_up": nrm(ks[16], (N_DENSE, D_MODEL, D_FF), D_MODEL ** -0.5),
        "dense_w_down": nrm(ks[17], (N_DENSE, D_FF, D_MODEL), D_FF ** -0.5),
        "moe_w_router": nrm(ks[18], (N_MOE, D_MODEL, N_EXPERTS), D_MODEL ** -0.5),
        "moe_w_gate": nrm(ks[19], (N_MOE, N_EXPERTS, D_MODEL, D_FF), D_MODEL ** -0.5),
        "moe_w_up": nrm(ks[20], (N_MOE, N_EXPERTS, D_MODEL, D_FF), D_MODEL ** -0.5),
        "moe_w_down": nrm(ks[21], (N_MOE, N_EXPERTS, D_FF, D_MODEL), D_FF ** -0.5),
        "final_norm_w": gain(ks[22], (D_MODEL,)),
    }

def reference(x, norm_mix_w, w_in, fox_f_bias, ret_gn_w, mla_q_norm_w, mla_kv_norm_w,
              mla_w_uq, mla_w_uk, mla_w_uv, w_br_fox, w_br_ret, w_br_mla, w_out,
              norm_ffn_w, dense_w_gate, dense_w_up, dense_w_down,
              moe_w_router, moe_w_gate, moe_w_up, moe_w_down, final_norm_w):
    for l in range(DEPTH):
        h = rmsnorm(x, norm_mix_w[l])
        x = x + hybrid_mixer(h, w_in[l], fox_f_bias[l], ret_gn_w[l], mla_q_norm_w[l],
                             mla_kv_norm_w[l], mla_w_uq[l], mla_w_uk[l], mla_w_uv[l],
                             w_br_fox[l], w_br_ret[l], w_br_mla[l], w_out[l])
        h = rmsnorm(x, norm_ffn_w[l])
        if l % 2 == 0:
            i = l // 2
            x = x + swiglu(h, dense_w_gate[i], dense_w_up[i], dense_w_down[i])
        else:
            i = l // 2
            x = x + moe_swiglu(h, moe_w_router[i], moe_w_gate[i], moe_w_up[i], moe_w_down[i])
    return rmsnorm(x, final_norm_w)


_drawn_inputs = setup_inputs


def setup_inputs(seed=0):
    import zlib

    import numpy as np

    out = dict(_drawn_inputs(seed))
    spreads = {}
    factors = {}
    for name, (base, spread) in spreads.items():
        noise = np.random.default_rng([zlib.crc32(name.encode()), seed]).standard_normal(out[name].shape)
        drawn = base * np.exp(spread * noise) if base else spread * noise
        out[name] = __import__('jax').numpy.asarray(drawn.astype(out[name].dtype))
    for name, factor in factors.items():
        out[name] = (out[name] * factor).astype(out[name].dtype)
    return out
```

```python
from contextlib import ExitStack

import numpy as np
import concourse.bass as bass
from concourse import mybir

F32 = mybir.dt.float32
F32R = mybir.dt.float32r
I32 = mybir.dt.int32
ALU = mybir.AluOpType
ACT = mybir.ActivationFunctionType
AX = mybir.AxisListType

P = 128
D = 1024
SEQ = 256
DEPTH = 2
HEADS = 8
FOX_D = 64
RET_K, RET_V = 64, 128
Q_RANK, KV_RANK = 384, 256
NOPE, ROPE = 64, 32
QK = NOPE + ROPE
D_FF = 3584
N_EXPERTS = 8
EPS = 1e-6
THETA = 10000.0
NB = SEQ // P
KC = D // P
MASKED = -1e30

WIDTHS = dict(fq=512, fk=512, fv=512, ff=8, rq=512, rk=512, rv=1024, rg=1024,
              cq=Q_RANK, ckv=KV_RANK, kr=ROPE, gl=3 * D)
START = {}
_at = 0
for _name, _w in WIDTHS.items():
    START[_name] = _at
    _at += _w
D_IN = _at

CONST_PARTS = dict(ident=P, causal=2 * P, cum=2 * P, decay=HEADS * 2 * P, ret_cos=NB * RET_K,
                   ret_sin=NB * RET_K, mla_cos=NB * ROPE, mla_sin=NB * ROPE, iota=P,
                   before=N_EXPERTS * N_EXPERTS)
CONST_AT = {}
_at = 0
for _name, _w in CONST_PARTS.items():
    CONST_AT[_name] = _at
    _at += _w
N_CONST = _at

N_PARAM = 2 * DEPTH * KC + DEPTH * KC + DEPTH * (Q_RANK + KV_RANK) // P
PARAM_AT = dict(mix=0, ffn=DEPTH * KC, gn=2 * DEPTH * KC, qn=3 * DEPTH * KC,
                kvn=3 * DEPTH * KC + DEPTH * Q_RANK // P)


def shape_constants():
    c = np.zeros((P, N_CONST), np.float32)

    def put(name, a):
        c[:, CONST_AT[name]:CONST_AT[name] + CONST_PARTS[name]] = a.reshape(P, -1)

    i = np.arange(P)
    put("ident", np.eye(P, dtype=np.float32))
    put("causal", np.concatenate([np.zeros((P, P)), np.where(i[None] <= i[:, None], 0.0, MASKED)], 1))
    put("cum", (i[:, None] <= np.arange(2 * P)[None]).astype(np.float32))
    gamma = 1.0 - 2.0 ** (-5.0 - np.arange(HEADS, dtype=np.float64))
    gap = np.arange(2 * P)[None] - i[:, None]
    decay = np.where(gap[:, None] >= 0, np.exp(np.maximum(gap, 0)[:, None] * np.log(gamma)[None, :, None]), 0.0)
    put("decay", decay * RET_K ** -0.5)
    for name, d in (("ret", RET_K), ("mla", ROPE)):
        inv = np.float32(THETA) ** (-np.arange(0, d, 2, dtype=np.float32) / np.float32(d))
        ang = (np.arange(SEQ, dtype=np.float32)[:, None] * inv.astype(np.float32)[None]).astype(np.float32)
        cos, sin = np.cos(ang), np.sin(ang)
        put(name + "_cos", np.concatenate([cos, cos], 1).reshape(NB, P, d).transpose(1, 0, 2))
        put(name + "_sin", np.concatenate([-sin, sin], 1).reshape(NB, P, d).transpose(1, 0, 2))
    put("iota", np.broadcast_to(i[None], (P, P)))
    e = np.arange(N_EXPERTS)
    put("before", np.broadcast_to((e[None, :] < e[:, None]).astype(np.float32), (P, N_EXPERTS, N_EXPERTS)))
    return c


GCOLS = 2048
MIX_RING = 4
FFN_RING = 6
PAIR_RING = 3
AHEAD = 2
FT = 512
N_FT = D_FF // FT
DENSE_STEP = 6
N_DENSE_TURNS = D_FF // 256 // 2
EXPERT_G = 6 * N_FT


def mixer_plan():
    steps = []

    def project(tile, n, sides=()):
        sides = list(sides)
        for j in range(n):
            steps.append(("granule", tile, j, j == n - 1))
            if sides:
                for s in sides.pop(0):
                    steps.append(("side",) + s)

    def side(what, k=0):
        steps.append(("side", what, k))

    def turn(tile):
        steps.append(("turn", tile))

    side("norm_mix")
    turn("norm0")
    turn("norm1")
    project("fq", 2)
    project("ff", 1)
    project("cq", 2)
    project("ckvkr", 2)
    side("forget")
    project("fk", 2)
    side("latent_norm")
    project("fv", 2)
    side("cumulate")
    turn("cqT")
    turn("ckvT")
    sm = lambda k: ("softmax", k)
    project("uq0", 1, [[sm(0)]])
    project("uq1", 1, [[sm(1)]])
    side("mla_rope_q")
    project("uk", 1, [[sm(2)]])
    side("mla_make_k")
    project("uv", 1, [[sm(3)]])
    project("rq", 2, [[sm(4)], [sm(5)]])
    side("ret_rope_q")
    project("rk", 2, [[sm(6)], [sm(7)]])
    side("ret_rope_k")
    for t in ("mqT0", "mqT1", "mkT0", "mkT1"):
        turn(t)
    project("rv0", 2, [[sm(8)], [sm(9)]])
    project("rv1", 2, [[sm(10)], [sm(11)]])
    turn("rqT")
    project("rg0", 2, [[sm(12)], [sm(13)]])
    turn("rkT")
    project("rg1", 2, [[sm(14)], [sm(15)]])
    ret = lambda k: ("retention", k)
    project("gate00", 2, [[sm(16), ret(0)], [sm(17), ret(1)]])
    project("gate10", 2, [[ret(2)], [ret(3)]])
    project("gate20", 2, [[ret(4)], [ret(5)]])
    project("fox0", 1, [[ret(6)]])
    project("mla0", 1, [[ret(7)]])
    project("gate01", 2, [[ret(8)], [("ret_norm", 0)]])
    project("gate11", 2)
    project("gate21", 2)
    project("fox1", 1)
    project("mla1", 1)
    turn("oretT0")
    turn("oretT1")
    project("ret0", 2)
    project("ret1", 2)
    turn("mergedT0")
    turn("mergedT1")
    project("out0", 2)
    project("out1", 2)
    side("norm_ffn")
    turn("ffn0")
    turn("ffn1")
    return steps


PLAN = mixer_plan()

TAKEN_BY_ACT_ALONE = ("rg0", "rg1", "gate")
TAKEN_BY_DVE_ALONE = ("fox", "ret", "mla", "out")


def takers(tile):
    if tile.startswith(TAKEN_BY_ACT_ALONE):
        return 1, 0
    if tile[:-1] in TAKEN_BY_DVE_ALONE:
        return 0, 1
    return 1, 1


class Tiles:

    def __init__(self):
        self.number, self.act, self.dve = {}, [], []
        a = d = 0
        for layer in range(DEPTH):
            for step in PLAN:
                if step[0] == "turn" or (step[0] == "granule" and step[2] == 0):
                    self.number[layer, step[1]] = len(self.act)
                    by_act, by_dve = takers(step[1])
                    a, d = a + by_act, d + by_dve
                    self.act.append(a)
                    self.dve.append(d)


TILES = Tiles()


def numbered(keys_of):
    number = {}
    for layer in range(DEPTH):
        for step in PLAN:
            for key in keys_of(step):
                number[(layer,) + key] = len(number)
    return number


def scores_in(step):
    if step[0] == "side" and (step[1], step[2] < (16 if step[1] == "softmax" else HEADS)) in (
            ("softmax", True), ("retention", True)):
        yield step[1:]


def right_in(step):
    if step[1] == "cumulate":
        yield "cumulate", 0
    elif step[1] == "softmax" and 1 <= step[2] < 17 or step[1] == "retention" and step[2]:
        yield step[1], step[2] - 1


USE_OF_6 = numbered(scores_in)
USE_OF_7 = numbered(right_in)
TURNS = numbered(lambda step: [step[1:]] if step[0] == "turn" else [])


def use_of_6(layer, what, k):
    return USE_OF_6[layer, what, k]


def use_of_7(layer, what, k):
    return USE_OF_7[layer, what, k]


def turn_count(layer, tile):
    return TURNS[layer, tile] + 1


def gate_slot(tile):
    branch, half = int(tile[4]), int(tile[5])
    return (branch + 3 * half) % 5


MISC_USES = 1 + N_FT + 4
MISC_ACT = 1 + N_FT
MISC_DVE = N_FT + 4
LOGITS, EXPS, CHOSEN, BEATEN, WEIGHTS, RANKS = range(6)
MIX_G = sum(s[0] == "granule" for s in PLAN)
G_MIX = [0, MIX_G + N_DENSE_TURNS * DENSE_STEP]
G_DENSE = MIX_G
G_MOE = G_MIX[1] + MIX_G
N_GRANULES = G_MOE + 2 * N_EXPERTS * EXPERT_G


class Stream:

    def __init__(self):
        self.slot, self.loads, self.before = [], [], []
        loads, last = [0] * FFN_RING, [None] * FFN_RING
        for g in range(N_GRANULES):
            if g < G_DENSE:
                s = g % MIX_RING
            elif g < G_MIX[1]:
                s = (g - G_DENSE) % FFN_RING
            elif g < G_MOE:
                s = (g - G_MIX[1]) % MIX_RING
            else:
                s = (g - G_MOE) % FFN_RING
            loads[s] += 1
            self.slot.append(s)
            self.loads.append(loads[s])
            self.before.append(last[s])
            last[s] = g


STREAM = Stream()


def expert_order():
    order = []
    for i in range(N_FT + 1):
        if i < N_FT:
            order += [("gate", i, 0), ("gate", i, 1), ("up", i, 0), ("up", i, 1)]
        if i > 0:
            order += [("down", i - 1, 0), ("down", i - 1, 1)]
    return order


EXPERT_ORDER = expert_order()


def build(nc, x, norm_mix_w, w_in, fox_f_bias, ret_gn_w, mla_q_norm_w, mla_kv_norm_w, mla_w_uq,
          mla_w_uk, mla_w_uv, w_br_fox, w_br_ret, w_br_mla, w_out, norm_ffn_w, dense_w_gate,
          dense_w_up, dense_w_down, moe_w_router, moe_w_gate, moe_w_up, moe_w_down, final_norm_w,
          consts, out):
    ctx = ExitStack()

    def sb(name, shape, dtype=F32):
        return ctx.enter_context(nc.sbuf_tensor(name, shape, dtype))

    def sem(name):
        return ctx.enter_context(nc.semaphore(name))

    with ctx:
        x_sb = sb("x_sb", [P, NB, D])
        cst = sb("cst", [P, N_CONST])
        param_T = sb("param_T", [P, N_PARAM])
        hT_hi = sb("hT_hi", [P, KC, SEQ], F32R)
        hT_lo = sb("hT_lo", [P, KC, SEQ], F32R)
        raw_low = sb("raw_low", [P, MIX_RING, GCOLS])
        w_hi = sb("w_hi", [P, PAIR_RING, GCOLS], F32R)
        w_lo = sb("w_lo", [P, PAIR_RING, GCOLS], F32R)
        forget_bias = sb("forget_bias", [P, DEPTH, HEADS])
        router_raw = sb("router_raw", [P, KC, N_EXPERTS])
        router_hi = sb("router_hi", [P, KC, N_EXPERTS], F32R)
        router_lo = sb("router_lo", [P, KC, N_EXPERTS], F32R)
        stat = sb("stat", [P, 64])
        eps_col = sb("eps_col", [P, 1])
        zeros = sb("zeros", [P, P])
        ARENA = 83 * 1024
        arena = sb("arena", [P, ARENA // 4])
        base = nc.sbuf_base - ARENA
        used = {}

        def at(region, offset, name, shape, dtype=F32):
            size = 4 * int(np.prod(shape[1:]))
            used[region] = max(used.get(region, 0), offset + size)
            start = dict(A=0, B=16384, C=28672, D=40960, R=57344, E=65536, X=0)[region]
            assert start + offset + size <= ARENA, (name, start + offset + size)
            return nc.alloc_sbuf_tensor_at(name, shape, dtype, offset=base + start + offset)

        K = 1024
        normed = at("A", 0, "normed", [P, NB, D])
        cq = at("A", 0, "cq", [P, NB, Q_RANK])
        ckvkr = at("A", 3 * K, "ckvkr", [P, NB, KV_RANK + ROPE])
        cqT_hi = at("A", 5632, "cqT_hi", [P, Q_RANK // P, SEQ], F32R)
        cqT_lo = at("A", 5632 + 3 * K, "cqT_lo", [P, Q_RANK // P, SEQ], F32R)
        ckvT_hi = at("A", 5632 + 6 * K, "ckvT_hi", [P, KV_RANK // P, SEQ], F32R)
        ckvT_lo = at("A", 5632 + 8 * K, "ckvT_lo", [P, KV_RANK // P, SEQ], F32R)
        omlaT_hi = at("A", 0, "omlaT_hi", [P, 4, SEQ], F32R)
        omlaT_lo = at("A", 4 * K, "omlaT_lo", [P, 4, SEQ], F32R)
        mv = at("A", 12 * K, "mv", [P, NB, 512])
        o_ret = at("A", 8 * K, "o_ret", [P, NB, D])
        fqT = at("B", 0, "fqT", [P, 4, SEQ])
        fkT = at("B", 4 * K, "fkT", [P, 4, SEQ])
        fv = at("B", 8 * K, "fv", [P, NB, 512])
        rg = at("B", 0, "rg", [P, NB, D])
        mq = at("C", 0, "mq", [P, NB, HEADS, QK])
        mk = at("C", 6 * K, "mk", [P, NB, HEADS, QK])
        rv = at("C", 0, "rv", [P, NB, D])
        merged = [at("B", 8 * K, "merged0", [P, NB, 512]), at("C", 8 * K, "merged1", [P, NB, 512])]
        mqT = at("D", 0, "mqT", [P, HEADS, SEQ])
        mkT = at("D", 8 * K, "mkT", [P, HEADS, SEQ])
        gates = [at("D", 4 * K * i, f"gates{i}", [P, NB, 512]) for i in range(4)]
        gates.append(at("R", 4 * K, "gates4", [P, NB, 512]))
        turned = at("E", 0, "turned", [P, NB, HEADS, RET_K])
        log_f = at("D", 4 * K, "log_f", [P, NB, P])
        cum_T = at("D", 5 * K, "cum_T", [P, SEQ])
        neg_cum_T = at("D", 6 * K, "neg_cum_T", [P, SEQ])
        latent_scratch = at("C", 0, "latent_scratch", [P, 2 * NB, Q_RANK])
        params = at("C", 0, "params", [N_PARAM, P])
        rq = at("R", 0, "rq", [P, NB, HEADS, RET_K])
        rk = at("R", 4 * K, "rk", [P, NB, HEADS, RET_K])
        mixed = at("R", 0, "mixed", [P, NB, 512])
        rqT = at("E", 0, "rqT", [P, 4, SEQ])
        rkT = at("E", 4 * K, "rkT", [P, 4, SEQ])
        ofoxT_hi = at("E", 8 * K, "ofoxT_hi", [P, 4, SEQ], F32R)
        ofoxT_lo = at("E", 12 * K, "ofoxT_lo", [P, 4, SEQ], F32R)
        prob = at("E", 16 * K, "prob", [P, 2, 384])
        forget = sb("forget", [P, 4, NB, HEADS])
        bn = sb("bn", [P, HEADS, NB, 6])
        ret_stat = sb("ret_stat", [P, NB, HEADS, 2])
        ret_dev = sb("ret_dev", [P, NB, HEADS])
        prob_T = sb("prob_T", [P, 2, 384])
        raw_high = at("X", ARENA - 4 * GCOLS * 2, "raw_high", [P, FFN_RING - MIX_RING, GCOLS])
        d_silu = at("X", 0, "d_silu", [P, 2, 512])
        d_act = at("X", 4 * K, "d_act", [P, 2, 512])
        d_act_hi = at("X", 8 * K, "d_act_hi", [P, 2, 512], F32R)
        d_act_lo = at("X", 12 * K, "d_act_lo", [P, 2, 512], F32R)
        h_hi = at("X", 8 * K, "h_hi", [P, NB, D], F32R)
        h_lo = at("X", 16 * K, "h_lo", [P, NB, D], F32R)
        ffn_w_row = at("X", 24 * K, "ffn_w_row", [P, D])
        route = sb("route", [P, 16, 4])
        onehot = at("X", 28 * K, "onehot", [P, NB, P], F32R)
        onehot_T = at("X", 29 * K, "onehot_T", [P, SEQ], F32R)
        xg_hi = at("X", 30 * K, "xg_hi", [P, KC, P], F32R)
        xg_lo = at("X", 34 * K, "xg_lo", [P, KC, P], F32R)
        e_silu = at("X", 38 * K, "e_silu", [P, 2, FT])
        e_act = at("X", 42 * K, "e_act", [P, 2, FT])
        e_actT_hi = at("X", 46 * K, "e_actT_hi", [P, 2, 4, P], F32R)
        e_actT_lo = at("X", 50 * K, "e_actT_lo", [P, 2, 4, P], F32R)
        y_hi = at("X", 54 * K, "y_hi", [P, D], F32R)
        y_lo = at("X", 58 * K, "y_lo", [P, D], F32R)
        assert 62 * K <= ARENA - 4 * GCOLS * 2
        rt = at("X", 46 * K, "rt", [P, 6, NB, N_EXPERTS])
        pairs = at("X", 50 * K, "pairs", [P, 2, NB, N_EXPERTS, N_EXPERTS])
        final_row = at("X", 0, "final_row", [P, D])
        result = at("X", 8 * K, "result", [P, NB, D])
        final_scratch = at("X", 16 * K, "final_scratch", [P, NB, D])
        here = sb("here", [P, 4])
        most = sb("most", [P, 1], I32)
        ps = ctx.enter_context(nc.psum_tensor("ps", [P, 8, 512], F32))

        consts_in, small_in, x_in, rows_in, final_in = (sem(n) for n in (
            "consts_in", "small_in", "x_in", "rows_in", "final_in"))
        raw_in = [sem(f"raw_in{i}") for i in range(FFN_RING)]
        hi_split, lo_split = sem("hi_split"), sem("lo_split")
        granule_used = sem("granule_used")
        act_step, dve_step = sem("act_step"), sem("dve_step")
        params_turned, params_ready = sem("params_turned"), sem("params_ready")
        zeroed = sem("zeroed")
        router_hi_ready, router_lo_ready = sem("router_hi_ready"), sem("router_lo_ready")
        tile_act, tile_dve = sem("tile_act"), sem("tile_dve")
        turned_ready = sem("turned_ready")
        source_ready = sem("source_ready")
        deviation = sem("deviation")
        logits_abs, log_terms, forget_ready = sem("logits_abs"), sem("log_terms"), sem("forget_ready")
        scores_ready, scores_taken = sem("scores_ready"), sem("scores_taken")
        row_max_ready, prob_exp, prob_ready = sem("row_max_ready"), sem("prob_exp"), sem("prob_ready")
        right_ready, right_act, neg_cum_ready = sem("right_ready"), sem("right_act"), sem("neg_cum_ready")
        heads_ready, heads_act, heads_dve = sem("heads_ready"), sem("heads_act"), sem("heads_dve")
        x_summed, here_ready, final_sq = sem("x_summed"), sem("here_ready"), sem("final_sq")
        ret_var_ready, ret_dev_ready = sem("ret_var_ready"), sem("ret_dev_ready")
        h_wide_ready, h_hi_ready, h_lo_ready = sem("h_wide_ready"), sem("h_hi_ready"), sem("h_lo_ready")
        d_opened, d_silu_ready, d_act_ready = sem("d_opened"), sem("d_silu_ready"), sem("d_act_ready")
        d_hi_ready, d_lo_ready, d_summed = sem("d_hi_ready"), sem("d_lo_ready"), sem("d_summed")
        logits_ready, logit_max_ready, logit_exp = sem("logits_ready"), sem("logit_max_ready"), sem("logit_exp")
        chosen_ready, ranks_ready, route_ready = sem("chosen_ready"), sem("ranks_ready"), sem("route_ready")
        onehot_ready, gathered, xg_hi_ready, xg_lo_ready = (sem(n) for n in (
            "onehot_ready", "gathered", "xg_hi_ready", "xg_lo_ready"))
        e_silu_ready, e_act_ready = sem("e_silu_ready"), sem("e_act_ready")
        misc_ready, misc_act, misc_dve = sem("misc_ready"), sem("misc_act"), sem("misc_dve")
        y_hi_ready, y_lo_ready = sem("y_hi_ready"), sem("y_lo_ready")
        stored = sem("stored")

        def const(name, *dims):
            v = cst[:, CONST_AT[name]:CONST_AT[name] + CONST_PARTS[name]]
            if len(dims) == 1:
                v = v.rearrange("p (a b) -> p a b", a=dims[0])
            return v

        ident = const("ident")
        causal = const("causal")
        cum = const("cum")
        decay = const("decay", HEADS)
        iota = const("iota")

        def channel_weights(what, layer, n):
            first = PARAM_AT[what] + layer * n
            return [param_T[:, first + c:first + c + 1] for c in range(n)]

        def raw_slot(s):
            return raw_low[:, s] if s < MIX_RING else raw_high[:, s - MIX_RING]

        def pick(w, k0, n, c0, cols):
            return n, cols, w[k0 * P:(k0 + n) * P, c0:c0 + cols].rearrange("(k p) c -> p k c", p=P)

        def mixer_granule(layer, tile, j):
            w = w_in[layer]
            if tile in ("fq", "fk"):
                return pick(w, 0, 8, START[tile] + 256 * j, 256)
            if tile == "ff":
                return pick(w, 0, 8, START["ff"], HEADS)
            if tile in ("fv", "rq", "rk"):
                return pick(w, 4 * j, 4, START[tile], 512)
            if tile[:2] in ("rv", "rg"):
                return pick(w, 4 * j, 4, START[tile[:2]] + 512 * int(tile[2]), 512)
            if tile == "cq":
                return pick(w, 4 * j, 4, START["cq"], Q_RANK)
            if tile == "ckvkr":
                return pick(w, 4 * j, 4, START["ckv"], KV_RANK + ROPE)
            if tile.startswith("gate"):
                return pick(w, 4 * j, 4, START["gl"] + D * int(tile[4]) + 512 * int(tile[5]), 512)
            if tile[:2] == "uq":
                return pick(mla_w_uq[layer], 0, 3, 384 * int(tile[2]), 384)
            if tile == "uk":
                return pick(mla_w_uk[layer], 0, 2, 0, 512)
            if tile == "uv":
                return pick(mla_w_uv[layer], 0, 2, 0, 512)
            w = dict(fox=w_br_fox, ret=w_br_ret, mla=w_br_mla, out=w_out)[tile[:-1]][layer]
            return pick(w, 4 * j, 4, 512 * int(tile[-1]), 512)

        GRANULE = {}
        for layer in range(DEPTH):
            g = G_MIX[layer]
            for step in PLAN:
                if step[0] == "granule":
                    GRANULE[g] = mixer_granule(layer, step[1], step[2])
                    g += 1

        def dense_granule(p, turn):
            if p < 4:
                w = (dense_w_gate, dense_w_up)[p % 2]
                c0 = turn * 512 + 256 * (p // 2)
                return 8, 256, w[0, :, bass.ds(c0, 256)].rearrange("(k p) c -> p k c", p=P)
            r0 = turn * 512 + 256 * (p - 4)
            return 2, D, dense_w_down[0, bass.ds(r0, 256), :].rearrange("(k p) c -> p k c", p=P)

        def expert_granule(p, e):
            what, i, half = EXPERT_ORDER[p]
            if what == "down":
                rows = slice(FT * i + 256 * half, FT * i + 256 * (half + 1))
                return 2, D, moe_w_down[0, e, rows, :].rearrange("(k p) c -> p k c", p=P)
            w = moe_w_gate if what == "gate" else moe_w_up
            return 4, FT, w[0, e, 512 * half:512 * (half + 1), FT * i:FT * (i + 1)].rearrange(
                "(k p) c -> p k c", p=P)

        def width(g):
            return GRANULE[g][0] * GRANULE[g][1] if g in GRANULE else GCOLS

        def w_parts(g, cols):
            n = width(g) // cols
            return [w[:, g % PAIR_RING, 0:n * cols].rearrange("p (k c) -> p k c", k=n) for w in (w_hi, w_lo)]

        SOURCE_OF = dict(norm0=1, norm1=1, cqT=2, ckvT=2, mqT0=3, mqT1=3, mkT0=4, mkT1=4, rqT=6, rkT=6,
                         oretT0=7, oretT1=7, ffn0=8, ffn1=8)
        SOURCES = 8
        READS = dict(uq0="cqT", uq1="cqT", uk="ckvT", uv="ckvT")

        def operand(tile):
            if tile in READS:
                hi, lo = (cqT_hi, cqT_lo) if tile[:2] == "uq" else (ckvT_hi, ckvT_lo)
                return hi, lo, READS[tile]
            if tile[:-1] == "fox":
                return ofoxT_hi, ofoxT_lo, None
            if tile[:-1] == "mla":
                return omlaT_hi, omlaT_lo, None
            if tile[:-1] == "ret":
                return hT_hi, hT_lo, "oretT1"
            if tile[:-1] == "out":
                return hT_hi, hT_lo, "mergedT1"
            return hT_hi, hT_lo, "norm1"

        def head_rows(buffer, h, cols):
            return buffer[64 * (h % 2):64 * (h % 2) + 64, h // 2, cols]

        def token_dst(tile, b):
            if tile == "ff":
                return forget[:, 0, b, :], HEADS
            if tile[:2] in ("uq", "rv"):
                n, buffer = int(tile[2]), mq[:, b].rearrange("p h d -> p (h d)") if tile[:2] == "uq" else rv[:, b]
                cols = 384 if tile[:2] == "uq" else 512
                return buffer[:, cols * n:cols * (n + 1)], cols
            if tile in ("rq", "rk"):
                return (rq if tile == "rq" else rk)[:, b].rearrange("p h d -> p (h d)"), 512
            buffer = dict(cq=cq, ckvkr=ckvkr, fv=fv, uv=mv)[tile]
            return buffer[:, b], buffer.shape[2]

        def turn_sources(tile):
            if tile[:2] in ("mq", "mk"):
                src = mq if tile[:2] == "mq" else mk
                chunks, rows = [lambda b, h=h: src[:, b, h, :] for h in range(4 * int(tile[3]), 4 * int(tile[3]) + 4)], QK
            else:
                if tile[:-1] in ("norm", "ffn", "oretT"):
                    src, first, n = (o_ret if tile[:-1] == "oretT" else normed), 4 * int(tile[-1]), 4
                elif tile[:-1] == "mergedT":
                    src, first, n = merged[int(tile[-1])], 0, 4
                else:
                    src, first, n = dict(cqT=(cq, 0, 3), ckvT=(ckvkr, 0, 2), rqT=(rq, 0, 4), rkT=(rk, 0, 4))[tile]
                by_token = (lambda b: src[:, b].rearrange("p h d -> p (h d)")) if src in (rq, rk) else (lambda b: src[:, b])
                chunks, rows = [lambda b, c=c: by_token(b)[:, P * c:P * (c + 1)] for c in range(first, first + n)], P
            return [(chunk(b), b, rows) for chunk in chunks for b in range(NB)]

        def turn_target(layer, tile):
            if tile == "cqT":
                return cqT_hi, cqT_lo, channel_weights("qn", layer, 3), 0, 3
            if tile == "ckvT":
                return ckvT_hi, ckvT_lo, channel_weights("kvn", layer, 2), 0, 2
            what = dict(norm="mix", ffn="ffn", oretT="gn", mergedT=None).get(tile[:-1], "plain")
            if what == "plain":
                return None, None, None, 0, 4
            first = 4 * int(tile[-1])
            weights = channel_weights(what, layer, KC)[first:first + 4] if what else None
            return hT_hi, hT_lo, weights, first, 4

        def plain_target(tile):
            if tile[:3] in ("mqT", "mkT"):
                first = 4 * int(tile[3])
                return (mqT if tile[:3] == "mqT" else mkT)[:, first:first + 4], QK
            return (rqT if tile == "rqT" else rkT)[:], P

        block = ctx.enter_context(nc.Block())

        @block.sync
        def _(sp):
            sp.dma_start(cst[:], consts).then_inc(consts_in, 16)
            sp.dma_start(x_sb[:], x.rearrange("a (b p) d -> p (a b) d", p=P)).then_inc(x_in, 16)
            at_row = 0
            for w in (norm_mix_w, norm_ffn_w, ret_gn_w, mla_q_norm_w, mla_kv_norm_w):
                rows = w.rearrange("l (c p) -> (l c) p", p=P)
                n = rows.shape[0]
                sp.dma_start(params[at_row:at_row + n, :], rows).then_inc(small_in, 16)
                at_row += n
            sp.dma_start(forget_bias[:].rearrange("p l h -> p (l h)"),
                         fox_f_bias.rearrange("l h -> (l h)").partition_broadcast(P)).then_inc(small_in, 16)
            sp.dma_start(router_raw[:], moe_w_router[0].rearrange("(k p) e -> p k e", p=P)).then_inc(small_in, 16)

            def load(g, granule, loaded_before=None):
                s = STREAM.slot[g]
                n, cols, source = granule
                sp.dma_start(raw_slot(s)[:, 0:n * cols].rearrange("p (k c) -> p k c", k=n),
                             source).then_inc(raw_in[s], 16)

            def mixer(layer):
                for g in range(G_MIX[layer], G_MIX[layer] + MIX_G):
                    if STREAM.before[g] is not None:
                        sp.wait_ge(lo_split, STREAM.before[g] + 1)
                    load(g, GRANULE[g])

            mixer(0)
            for p in range(DENSE_STEP):
                if p < MIX_RING:
                    sp.wait_ge(lo_split, STREAM.before[G_DENSE + p] + 1)
                else:
                    sp.wait_ge(source_ready, SOURCES)
                load(G_DENSE + p, dense_granule(p, 0))
            with sp.Fori(1, N_DENSE_TURNS) as turn:
                for p in range(DENSE_STEP):
                    sp.wait_ge(lo_split, G_DENSE + p + 1 - DENSE_STEP + turn * DENSE_STEP)
                    load(G_DENSE + p, dense_granule(p, turn))
            mixer(1)
            def expert_loads(e, E, first=False):
                for p in range(EXPERT_G):
                    g = G_MOE + p
                    if first and p < MIX_RING:
                        sp.wait_ge(lo_split, STREAM.before[g] + 1)
                    elif first and p < FFN_RING:
                        if p == MIX_RING:
                            sp.wait_ge(source_ready, 2 * SOURCES)
                            sp.dma_start(ffn_w_row[:], norm_ffn_w[1].partition_broadcast(P)).then_inc(rows_in, 16)
                    else:
                        sp.wait_ge(lo_split, g + 1 - FFN_RING + E * EXPERT_G)
                    load(g, expert_granule(p, e))

            expert_loads(0, 0, first=True)
            with sp.Fori(1, N_EXPERTS) as e:
                expert_loads(e, e)
            sp.wait_ge(route_ready, 1)
            many = sp.value_load(most[0:1, 0:1], min_val=0, max_val=SEQ)
            with sp.If(many > P):
                with sp.Fori(0, N_EXPERTS) as e:
                    expert_loads(e, e + N_EXPERTS)
            sp.wait_ge(final_in, 1)
            sp.dma_start(final_row[:], final_norm_w.partition_broadcast(P)).then_inc(rows_in, 16)
            sp.wait_ge(final_in, 2)
            sp.dma_start(out.rearrange("a (b p) d -> p (a b) d", p=P), result[:]).then_inc(stored, 16)
            sp.wait_ge(stored, 16)

        @block.tensor
        def _(pe):
            mm = nc.tensor.matmul

            def three(dst, sides, moving, start, stop):
                mm(dst, sides[0], moving[0], start=start, stop=False)
                mm(dst, sides[0], moving[1], start=False, stop=False)
                return mm(dst, sides[1], moving[0], start=False, stop=stop)

            def split_arrived(g):
                pe.wait_ge(hi_split, g + 1)
                pe.wait_ge(lo_split, g + 1)

            def tile_done(layer, tile):
                n = TILES.number[layer, tile]
                if TILES.act[n]:
                    pe.wait_ge(tile_act, TILES.act[n])
                if TILES.dve[n]:
                    pe.wait_ge(tile_dve, TILES.dve[n])

            def banks_free(layer, tile):
                n = TILES.number[layer, tile] - 2
                if n >= 0:
                    if TILES.act[n]:
                        pe.wait_ge(tile_act, TILES.act[n])
                    if TILES.dve[n]:
                        pe.wait_ge(tile_dve, TILES.dve[n])

            def granule(layer, g, tile, j, last):
                bank = 2 * (TILES.number[layer, tile] % 2)
                hi, lo, ready = operand(tile)
                n, cols, _ = GRANULE[g]
                if j == 0:
                    banks_free(layer, tile)
                    if ready:
                        tile_done(layer, ready)
                    if tile[:-1] == "fox":
                        pe.wait_ge(heads_act, 4 * layer + 2)
                        pe.wait_ge(heads_dve, 4 * layer + 2)
                    if tile[:-1] == "mla":
                        pe.wait_ge(heads_act, 4 * layer + 4)
                        pe.wait_ge(heads_dve, 4 * layer + 4)
                split_arrived(g)
                wh, wl = w_parts(g, cols)
                if tile in ("fq", "fk"):
                    for c in range(2):
                        for k in range(n):
                            i = three(ps[:, bank + j, SEQ * c:SEQ * (c + 1)],
                                      [w[:, k, P * c:P * (c + 1)] for w in (wh, wl)],
                                      (hi[:, k, :], lo[:, k, :]), k == 0, k == n - 1)
                else:
                    for b in range(NB):
                        for k in range(n):
                            kk = 4 * j + k
                            i = three(ps[:, bank + b, 0:cols], [s[:, kk, P * b:P * (b + 1)] for s in (hi, lo)],
                                      (wh[:, k, :], wl[:, k, :]), kk == 0, last and k == n - 1)
                i.then_inc(granule_used, 1)

            def turn(layer, tile):
                banks_free(layer, tile)
                if tile[:-1] == "mergedT":
                    tile_done(layer, "ret1")
                else:
                    pe.wait_ge(source_ready, SOURCES * layer + SOURCE_OF[tile])
                bank = 2 * (TILES.number[layer, tile] % 2)
                for c, (src, b, rows) in enumerate(turn_sources(tile)):
                    i = nc.tensor.transpose(ps[0:rows, bank + c // 4, P * (c % 4):P * (c % 4 + 1)], src, ident)
                i.then_inc(turned_ready, 1)

            def scores(layer, k):
                h = k % HEADS
                fox = k < HEADS
                if use_of_6(layer, "softmax", k):
                    pe.wait_ge(scores_taken, use_of_6(layer, "softmax", k))
                if k == 0:
                    tile_done(layer, "fq")
                    tile_done(layer, "fk")
                    pe.wait_ge(neg_cum_ready, layer + 1)
                if k == HEADS:
                    tile_done(layer, "mkT1")
                for b in range(NB):
                    keys = P * (b + 1)
                    dst = ps[:, 6, P * b:P * b + keys]
                    queries = slice(P * b, P * (b + 1))
                    if fox:
                        mm(dst, head_rows(fqT, h, queries), head_rows(fkT, h, slice(0, keys)),
                           start=True, stop=False)
                        pick_h = ident[:, h:h + 1]
                        mm(dst, cum_T[:, queries], pick_h.broadcast_to([P, keys]), start=False, stop=False)
                        i = mm(dst, pick_h.broadcast_to([P, P]), neg_cum_T[:, 0:keys], start=False, stop=True)
                    else:
                        i = mm(dst, mqT[0:QK, h, queries], mkT[0:QK, h, 0:keys], start=True, stop=True)
                i.then_inc(scores_ready, 1)

            def turn_probs(layer, k):
                pe.wait_ge(prob_ready, 16 * layer + k + 1)
                free = use_of_7(layer, "softmax", k)
                if free:
                    pe.wait_ge(right_act, free)
                for c in range(3):
                    i = nc.tensor.transpose(ps[:, 7, P * c:P * (c + 1)], prob[:, k % 2, P * c:P * (c + 1)], ident)
                i.then_inc(right_ready, 1)

            def values(layer, k):
                h = k % HEADS
                unit = 4 * layer + k // 4
                if k % 4 == 0 and unit >= 2:
                    pe.wait_ge(heads_act, unit - 1)
                    pe.wait_ge(heads_dve, unit - 1)
                pe.wait_ge(right_act, use_of_7(layer, "softmax", k) + 1)
                if k == 0:
                    tile_done(layer, "fv")
                if k == HEADS:
                    tile_done(layer, "uv")
                v = fv if k < HEADS else mv
                dst = ps[64 * (h % 2):64 * (h % 2) + 64, 4 + unit % 2,
                         SEQ * (h // 2 % 2):SEQ * (h // 2 % 2 + 1)]
                vh = slice(64 * h, 64 * h + 64)
                pt = prob_T[:, k % 2]
                mm(dst[:, 0:P], v[:, 0, vh], pt[:, 0:P], start=True, stop=True)
                mm(dst[:, P:2 * P], v[:, 0, vh], pt[:, P:2 * P], start=True, stop=False)
                i = mm(dst[:, P:2 * P], v[:, 1, vh], pt[:, 2 * P:3 * P], start=False, stop=True)
                if k % 4 == 3:
                    i.then_inc(heads_ready, 1)

            def retention_scores(layer, r):
                pe.wait_ge(scores_taken, use_of_6(layer, "retention", r))
                if r == 0:
                    tile_done(layer, "rqT")
                    tile_done(layer, "rkT")
                mm(ps[:, 6, 0:SEQ], head_rows(rkT, r, slice(0, P)), head_rows(rqT, r, slice(0, SEQ)),
                   start=True, stop=True)
                mm(ps[:, 6, SEQ:SEQ + P], head_rows(rkT, r, slice(P, SEQ)), head_rows(rqT, r, slice(P, SEQ)),
                   start=True, stop=True).then_inc(scores_ready, 1)

            def retention_values(layer, r):
                pe.wait_ge(scores_taken, use_of_6(layer, "retention", r) + 1)
                pe.wait_ge(right_act, use_of_7(layer, "retention", r))
                if r == 0:
                    tile_done(layer, "rv1")
                pt = prob_T[:, r % 2]
                vh = slice(RET_V * r, RET_V * (r + 1))
                mm(ps[:, 7, 0:P], pt[:, 0:P], rv[:, 0, vh], start=True, stop=True)
                mm(ps[:, 7, P:2 * P], pt[:, P:2 * P], rv[:, 0, vh], start=True, stop=False)
                mm(ps[:, 7, P:2 * P], pt[:, 2 * P:3 * P], rv[:, 1, vh], start=False, stop=True).then_inc(right_ready, 1)

            def side(layer, what, k):
                if what == "cumulate":
                    pe.wait_ge(forget_ready, layer + 1)
                    free = use_of_7(layer, "cumulate", 0)
                    if free:
                        pe.wait_ge(right_act, free)
                    mm(ps[:, 7, 0:P], log_f[:, 0], cum[:, 0:P], start=True, stop=True)
                    mm(ps[:, 7, P:2 * P], log_f[:, 0], cum[:, P:2 * P], start=True, stop=False)
                    mm(ps[:, 7, P:2 * P], log_f[:, 1], cum[:, 0:P], start=False, stop=True).then_inc(right_ready, 1)
                elif what == "softmax":
                    if k < 16:
                        scores(layer, k)
                    if 1 <= k < 17:
                        turn_probs(layer, k - 1)
                    if k >= 2:
                        values(layer, k - 2)
                elif what == "retention":
                    if k < HEADS:
                        retention_scores(layer, k)
                    if k:
                        retention_values(layer, k - 1)

            def mixer(layer):
                g = G_MIX[layer]
                for step in PLAN:
                    if step[0] == "granule":
                        granule(layer, g, *step[1:])
                        g += 1
                    elif step[0] == "turn":
                        turn(layer, step[1])
                    else:
                        side(layer, *step[1:])

            pe.wait_ge(consts_in, 16)
            pe.wait_ge(small_in, 16 * 7)
            nc.tensor.transpose(ps[:, 4, 0:N_PARAM], params[:], ident[0:N_PARAM, 0:N_PARAM]).then_inc(params_turned, 1)
            pe.wait_ge(zeroed, 1)
            pe.wait_ge(params_ready, 1)
            mixer(0)

            tile_done(0, "ffn1")
            for bank in range(4, 8):
                mm(ps[:, bank, :], zeros[:], cst[:, 0:512], start=True, stop=False)
            with pe.Fori(0, N_DENSE_TURNS) as turn_no:
                g0 = turn_no * DENSE_STEP
                for p in range(DENSE_STEP):
                    g = G_DENSE + p
                    pe.wait_ge(hi_split, g0 + g + 1)
                    pe.wait_ge(lo_split, g0 + g + 1)
                    i2 = p // 2 if p < 4 else p - 4
                    if p < 4:
                        if p % 2 == 0:
                            pe.wait_ge(d_act_ready, turn_no * 2 + i2 + 1)
                        wh, wl = w_parts(g, 256)
                        for c in range(2):
                            for k in range(KC):
                                i = three(ps[:, p, SEQ * c:SEQ * (c + 1)],
                                          [w[:, k, P * c:P * (c + 1)] for w in (wh, wl)],
                                          (hT_hi[:, k, :], hT_lo[:, k, :]), k == 0, k == KC - 1)
                    else:
                        pe.wait_ge(d_hi_ready, turn_no * 2 + i2 + 1)
                        pe.wait_ge(d_lo_ready, turn_no * 2 + i2 + 1)
                        wh, wl = w_parts(g, D)
                        for c in range(2):
                            for b in range(NB):
                                for n in range(2):
                                    tok = slice(SEQ * c + P * b, SEQ * c + P * (b + 1))
                                    i = three(ps[:, 4 + 2 * b + n, :],
                                              (d_act_hi[:, i2, tok], d_act_lo[:, i2, tok]),
                                              (wh[:, c, 512 * n:512 * (n + 1)], wl[:, c, 512 * n:512 * (n + 1)]),
                                              False, False)
                    i.then_inc(granule_used, 1)
            for bank in range(4, 8):
                i = mm(ps[:, bank, :], zeros[:], cst[:, 0:512], start=False, stop=True)
            i.then_inc(d_summed, 1)
            mixer(1)

            tile_done(1, "ffn1")
            pe.wait_ge(router_hi_ready, 1)
            pe.wait_ge(router_lo_ready, 1)
            for b in range(NB):
                dst = ps[:, 4, N_EXPERTS * b:N_EXPERTS * (b + 1)]
                for k in range(KC):
                    tok = slice(P * b, P * (b + 1))
                    three(dst, (hT_hi[:, k, tok], hT_lo[:, k, tok]), (router_hi[:, k], router_lo[:, k]), k == 0, False)
                    i = mm(dst, hT_lo[:, k, tok], router_lo[:, k], start=False, stop=k == KC - 1)
            i.then_inc(logits_ready, 1)
            pe.wait_ge(chosen_ready, 1)
            chosen = [rt[:, CHOSEN, b] for b in range(NB)]
            own, whole = cum[:, 0:P], cum[:, P:2 * P]
            E8 = N_EXPERTS
            mm(ps[:, 5, 0:E8], own, chosen[0], start=True, stop=True)
            mm(ps[:, 5, E8:2 * E8], whole, chosen[0], start=True, stop=False)
            mm(ps[:, 5, E8:2 * E8], own, chosen[1], start=False, stop=True)
            mm(ps[:, 5, 2 * E8:3 * E8], whole, chosen[0], start=True, stop=False)
            mm(ps[:, 5, 2 * E8:3 * E8], whole, chosen[1], start=False, stop=True).then_inc(ranks_ready, 1)

            def expert(E):
                uses = [0]

                def misc_bank():
                    u = uses[0]
                    uses[0] += 1
                    pe.wait_ge(misc_act, E * MISC_ACT + (1 + min(max(u - 1, 0), MISC_ACT)))
                    pe.wait_ge(misc_dve, E * MISC_DVE + (1 + max(u - 2, 0)))
                    return 6 + u % 2

                pe.wait_ge(onehot_ready, E + 1)
                bank = misc_bank()
                for b in range(NB):
                    i = nc.tensor.transpose(ps[:, bank, P * b:P * (b + 1)], onehot.bitcast(F32)[:, b], ident)
                i.then_inc(misc_ready, 1)
                for part, h in enumerate((h_hi, h_lo)):
                    for k in range(KC):
                        for b in range(NB):
                            i = mm(ps[:, 2 * part + k // 4, P * (k % 4):P * (k % 4 + 1)],
                                   h[:, b, P * k:P * (k + 1)], onehot[:, b], start=b == 0, stop=b == NB - 1)
                i.then_inc(gathered, 1)
                pe.wait_ge(xg_hi_ready, E + 1)
                pe.wait_ge(xg_lo_ready, E + 1)

                def turn_act(i):
                    pe.wait_ge(e_act_ready, E * N_FT + (i + 1))
                    bank = misc_bank()
                    for c in range(4):
                        t = nc.tensor.transpose(ps[:, bank, P * c:P * (c + 1)], e_act[:, i % 2, P * c:P * (c + 1)], ident)
                    t.then_inc(misc_ready, 1)

                for p, (what, i, half) in enumerate(EXPERT_ORDER):
                    g = G_MOE + p
                    if what == "gate" and half == 0 and i >= 2:
                        pe.wait_ge(e_act_ready, E * N_FT + (i - 1))
                    if what == "down" and half == 0:
                        if i == N_FT - 1:
                            turn_act(i)
                        pe.wait_ge(misc_act, E * MISC_ACT + (1 + i + 2))
                        pe.wait_ge(misc_dve, E * MISC_DVE + (1 + i + 1))
                    pe.wait_ge(hi_split, E * EXPERT_G + (g + 1))
                    pe.wait_ge(lo_split, E * EXPERT_G + (g + 1))
                    if what == "down":
                        wh, wl = w_parts(g, D)
                        for c in range(2):
                            f = 2 * half + c
                            for n in range(2):
                                cols = slice(512 * n, 512 * (n + 1))
                                m = three(ps[:, 4 + n, :], (e_actT_hi[:, i % 2, f], e_actT_lo[:, i % 2, f]),
                                          (wh[:, c, cols], wl[:, c, cols]), i == 0 and f == 0,
                                          i == N_FT - 1 and f == 3)
                    else:
                        bank = 2 * (i % 2) + (what == "up")
                        wh, wl = w_parts(g, FT)
                        for k in range(4):
                            kk = 4 * half + k
                            m = three(ps[:, bank, :], (xg_hi[:, kk], xg_lo[:, kk]), (wh[:, k], wl[:, k]),
                                      kk == 0, kk == KC - 1)
                    m.then_inc(granule_used, 1)
                    if what == "gate" and half == 1 and i >= 1:
                        turn_act(i - 1)
                pe.wait_ge(y_hi_ready, E + 1)
                pe.wait_ge(y_lo_ready, E + 1)
                for b in range(NB):
                    for n in range(2):
                        bank = misc_bank()
                        cols = slice(512 * n, 512 * (n + 1))
                        tok = slice(P * b, P * (b + 1))
                        mm(ps[:, bank, :], onehot_T[:, tok], y_hi[:, cols], start=True, stop=False)
                        mm(ps[:, bank, :], onehot_T[:, tok], y_lo[:, cols], start=False, stop=True).then_inc(misc_ready, 1)

            pe.wait_ge(h_lo_ready, 1)
            with pe.Fori(0, N_EXPERTS) as e:
                expert(e)
            pe.wait_ge(route_ready, 1)
            many = pe.value_load(most[0:1, 0:1], min_val=0, max_val=SEQ)
            with pe.If(many > P):
                with pe.Fori(0, N_EXPERTS) as e:
                    expert(e + N_EXPERTS)

        @block.scalar
        def _(act):
            af = nc.scalar.activation
            steps = [0]

            def then(i):
                steps[0] += 1
                i.then_inc(act_step, 1)
                act.wait_ge(act_step, steps[0])

            def split(g, turn=0, loads=0, used=0):
                s = STREAM.slot[g]
                act.wait_ge(raw_in[s], turn * (16 * loads) + 16 * STREAM.loads[g])
                if g >= PAIR_RING:
                    act.wait_ge(granule_used, turn * used + (g - PAIR_RING + 1))
                n = width(g)
                af(w_hi[:, g % PAIR_RING, 0:n], raw_slot(s)[:, 0:n], ACT.Copy).then_inc(hi_split, 1)

            def deviations(pieces, dims):
                for i, (piece, scratch) in enumerate(pieces):
                    last = af(scratch, piece, ACT.Square, accum_out=stat[:, i:i + 1])
                then(last)
                for i, (n, dim) in enumerate(dims):
                    a = sum(m for m, _ in dims[:i])
                    last = af(stat[:, 16 + a:16 + a + n], stat[:, a:a + n], ACT.Sqrt, bias=eps_col[:],
                              scale=1.0 / dim)
                last.then_inc(deviation, 1)

            def tile_dve_done(layer, tile):
                act.wait_ge(tile_dve, TILES.dve[TILES.number[layer, tile]])

            def take(layer, tile, g):
                bank = 2 * (TILES.number[layer, tile] % 2)
                if not takers(tile)[0]:
                    return
                act.wait_ge(granule_used, g + 1)
                if tile == "fq":
                    i = af(fqT[:, 0:2], ps[:, bank].rearrange("p (c t) -> p c t", c=2), ACT.Copy, scale=FOX_D ** -0.5)
                elif tile == "fk":
                    i = af(fkT[:, 0:2], ps[:, bank].rearrange("p (c t) -> p c t", c=2), ACT.Copy)
                elif tile == "uk":
                    i = af(mk[:, 0, :, 0:NOPE], ps[:, bank].rearrange("p (h d) -> p h d", h=HEADS), ACT.Copy)
                elif tile in ("rg0", "rg1"):
                    n = int(tile[2])
                    i = af(rg[:, :, 512 * n:512 * (n + 1)], ps[:, bank:bank + 2, :], ACT.Silu)
                elif tile.startswith("gate"):
                    i = af(gates[gate_slot(tile)][:], ps[:, bank:bank + 2, :], ACT.Sigmoid)
                else:
                    dst, cols = token_dst(tile, 0)
                    i = af(dst, ps[:, bank, 0:cols], ACT.Copy)
                i.then_inc(tile_act, 1)

            def turned_tile(layer, tile):
                act.wait_ge(turned_ready, turn_count(layer, tile))
                bank = 2 * (TILES.number[layer, tile] % 2)
                hi, _, weights, first, n = turn_target(layer, tile)
                if weights is None and hi is None:
                    dst, rows = plain_target(tile)
                    i = af(dst[0:rows, 0:2], ps[0:rows, bank].rearrange("p (c t) -> p c t", c=2), ACT.Copy)
                else:
                    for c in range(n):
                        src = ps[:, bank + c // 2, SEQ * (c % 2):SEQ * (c % 2 + 1)]
                        if weights is None:
                            i = af(hi[:, first + c], src, ACT.Copy)
                        else:
                            i = af(hi[:, first + c], src, ACT.Copy, scale=weights[c])
                i.then_inc(tile_act, 1)

            def heads_split(layer, u):
                act.wait_ge(heads_ready, 4 * layer + u + 1)
                hi = ofoxT_hi if u < 2 else omlaT_hi
                af(hi[:, 2 * (u % 2):2 * (u % 2) + 2], ps[:, 4 + u % 2].rearrange("p (c t) -> p c t", c=2),
                   ACT.Copy).then_inc(heads_act, 1)

            def side(layer, what, k):
                if what in ("norm_mix", "norm_ffn"):
                    if what == "norm_mix" and layer == 0:
                        act.wait_ge(x_in, 16)
                    elif what == "norm_mix":
                        act.wait_ge(x_summed, 1)
                    else:
                        tile_dve_done(layer, "out1")
                    deviations([(x_sb[:, b], normed[:, b]) for b in range(NB)], [(NB, D)])
                elif what == "forget":
                    act.wait_ge(logits_abs, layer + 1)
                    then(af(forget[:, 2], forget[:, 1], ACT.Exp, scale=-1.0))
                    af(forget[:, 3], forget[:, 2], ACT.Ln, bias=1.0).then_inc(log_terms, 1)
                elif what == "latent_norm":
                    tile_dve_done(layer, "cq")
                    tile_dve_done(layer, "ckvkr")
                    act.wait_ge(tile_act, TILES.act[TILES.number[layer, "ckvkr"]])
                    deviations([(cq[:, b], latent_scratch[:, b]) for b in range(NB)]
                               + [(ckvkr[:, b, 0:KV_RANK], latent_scratch[:, NB + b, 0:KV_RANK]) for b in range(NB)],
                               [(NB, Q_RANK), (NB, KV_RANK)])
                elif what == "cumulate":
                    act.wait_ge(right_ready, use_of_7(layer, "cumulate", 0) + 1)
                    af(cum_T[:], ps[:, 7, 0:SEQ], ACT.Copy).then_inc(right_act, 1)
                elif what == "softmax":
                    if k < 16:
                        n = 16 * layer + k
                        act.wait_ge(row_max_ready, n + 1)
                        for b in range(NB):
                            cols = slice(P * b, P * b + P * (b + 1))
                            i = af(prob[:, k % 2, cols], prob[:, k % 2, cols], ACT.Exp,
                                   bias=stat[:, 34 + 2 * (k % 2) + b:35 + 2 * (k % 2) + b],
                                   accum_out=stat[:, 38 + 2 * (k % 2) + b:39 + 2 * (k % 2) + b])
                        i.then_inc(prob_exp, 1)
                    if 1 <= k < 17:
                        act.wait_ge(right_ready, use_of_7(layer, "softmax", k - 1) + 1)
                        af(prob_T[:, (k - 1) % 2], ps[:, 7, 0:384], ACT.Copy).then_inc(right_act, 1)
                    if k >= 2 and (k - 2) % 4 == 3:
                        heads_split(layer, (k - 2) // 4)
                elif what == "retention" and k:
                    act.wait_ge(right_ready, use_of_7(layer, "retention", k - 1) + 1)
                    af(o_ret[:, :, RET_V * (k - 1):RET_V * k], ps[:, 7, 0:SEQ].rearrange("p (b e) -> p b e", b=NB),
                       ACT.Copy).then_inc(right_act, 1)
                elif what == "ret_norm":
                    act.wait_ge(ret_var_ready, HEADS * (layer + 1))
                    af(ret_dev[:], ret_stat[:, :, :, 1], ACT.Sqrt, bias=eps_col[:]).then_inc(ret_dev_ready, 1)

            def mixer(layer):
                g = G_MIX[layer]
                if layer == 0:
                    for first in range(AHEAD):
                        split(first)
                for step in PLAN:
                    if step[0] == "granule":
                        if g + AHEAD < G_MOE:
                            split(g + AHEAD)
                        if step[3]:
                            take(layer, step[1], g)
                        g += 1
                    elif step[0] == "turn":
                        turned_tile(layer, step[1])
                    else:
                        side(layer, *step[1:])

            act.wait_ge(zeroed, 1)
            act.wait_ge(small_in, 16 * 7)
            af(router_hi[:], router_raw[:], ACT.Copy).then_inc(router_hi_ready, 1)
            act.wait_ge(params_turned, 1)
            af(param_T[:], ps[:, 4, 0:N_PARAM], ACT.Copy).then_inc(params_ready, 1)
            act.wait_ge(params_ready, 1)
            mixer(0)

            with act.Fori(0, N_DENSE_TURNS) as turn_no:
                def silu(i):
                    act.wait_ge(granule_used, turn_no * DENSE_STEP + (G_DENSE + 2 * i + 1))
                    af(d_silu[:, i], ps[:, 2 * i, :], ACT.Silu).then_inc(d_silu_ready, 1)

                def hi_part(i):
                    act.wait_ge(d_act_ready, turn_no * 2 + (i + 3))
                    af(d_act_hi[:, i], d_act[:, i], ACT.Copy).then_inc(d_hi_ready, 1)

                for p in range(DENSE_STEP):
                    split(G_DENSE + p + AHEAD, turn_no, 1, DENSE_STEP)
                    if p == 0:
                        silu(0)
                    if p == 2:
                        hi_part(0)
                        silu(1)
                    if p == 4:
                        hi_part(1)
            mixer(1)

            act.wait_ge(h_wide_ready, 1)
            af(h_hi[:], normed[:], ACT.Copy).then_inc(h_hi_ready, 1)
            act.wait_ge(logit_max_ready, 1)
            for b in range(NB):
                i = af(rt[:, EXPS, b], rt[:, LOGITS, b], ACT.Exp, bias=stat[:, 44 + b:45 + b])
            i.then_inc(logit_exp, 1)

            def expert(E):
                def turned_hi(i):
                    act.wait_ge(misc_ready, E * MISC_USES + (i + 2))
                    af(e_actT_hi[:, i % 2].rearrange("p a b -> p (a b)"), ps[:, 6 + (i + 1) % 2, :],
                       ACT.Copy).then_inc(misc_act, 1)

                for p in range(AHEAD):
                    split(G_MOE + p, E, EXPERT_G // FFN_RING, EXPERT_G)
                act.wait_ge(misc_ready, E * MISC_USES + 1)
                af(onehot_T[:], ps[:, 6, 0:SEQ], ACT.Copy).then_inc(misc_act, 1)
                act.wait_ge(gathered, E + 1)
                af(xg_hi[:].rearrange("p (a k) t -> p a (k t)", a=2), ps[:, 0:2, :], ACT.Copy).then_inc(xg_hi_ready, 1)
                for p, (what, i, half) in enumerate(EXPERT_ORDER):
                    if p + AHEAD < EXPERT_G:
                        split(G_MOE + p + AHEAD, E, EXPERT_G // FFN_RING, EXPERT_G)
                    if what == "gate" and half == 1:
                        act.wait_ge(granule_used, E * EXPERT_G + (G_MOE + p + 1))
                        af(e_silu[:, i % 2], ps[:, 2 * (i % 2), :], ACT.Silu).then_inc(e_silu_ready, 1)
                        if i >= 1:
                            turned_hi(i - 1)
                    if what == "down" and half == 1 and i == N_FT - 2:
                        turned_hi(N_FT - 1)
                act.wait_ge(granule_used, E * EXPERT_G + (G_MOE + EXPERT_G))
                af(y_hi[:].rearrange("p (a c) -> p a c", a=2), ps[:, 4:6, :], ACT.Copy).then_inc(y_hi_ready, 1)

            act.sem_inc(misc_act, 1)
            with act.Fori(0, N_EXPERTS) as e:
                expert(e)
            act.wait_ge(route_ready, 1)
            many = act.value_load(most[0:1, 0:1], min_val=0, max_val=SEQ)
            with act.If(many > P):
                with act.Fori(0, N_EXPERTS) as e:
                    expert(e + N_EXPERTS)
            act.wait_ge(final_in, 1)
            for b in range(NB):
                last = af(final_scratch[:, b], x_sb[:, b], ACT.Square, accum_out=stat[:, b:b + 1])
            last.then_inc(final_sq, 1)
            act.wait_ge(final_sq, 1)
            af(stat[:, 16:16 + NB], stat[:, 0:NB], ACT.Sqrt, bias=eps_col[:], scale=1.0 / D).then_inc(deviation, 1)

        @block.vector
        def _(dve):
            v = nc.vector
            steps = [0]

            def then(i):
                steps[0] += 1
                i.then_inc(dve_step, 1)
                dve.wait_ge(dve_step, steps[0])

            def split(g, turn=0, loads=0, used=0):
                s = STREAM.slot[g]
                dve.wait_ge(hi_split, turn * used + (g + 1))
                n = width(g)
                v.tensor_tensor(w_lo[:, g % PAIR_RING, 0:n], raw_slot(s)[:, 0:n],
                                w_hi.bitcast(F32)[:, g % PAIR_RING, 0:n], ALU.subtract).then_inc(lo_split, 1)

            norms = [0]

            def scales(n):
                norms[0] += 1
                dve.wait_ge(deviation, norms[0])
                then(v.reciprocal(stat[:, 24:24 + n], stat[:, 16:16 + n]))

            def tile_act_done(layer, tile):
                dve.wait_ge(tile_act, TILES.act[TILES.number[layer, tile]])

            def take(layer, tile, g):
                bank = 2 * (TILES.number[layer, tile] % 2)
                if not takers(tile)[1]:
                    return
                dve.wait_ge(granule_used, g + 1)
                if tile == "fq":
                    i = v.tensor_scalar(fqT[:, 2:4], ps[:, bank + 1].rearrange("p (c t) -> p c t", c=2),
                                        FOX_D ** -0.5, None, ALU.mult)
                elif tile == "fk":
                    i = v.tensor_copy(fkT[:, 2:4], ps[:, bank + 1].rearrange("p (c t) -> p c t", c=2))
                elif tile == "uk":
                    i = v.tensor_copy(mk[:, 1, :, 0:NOPE], ps[:, bank + 1].rearrange("p (h d) -> p h d", h=HEADS))
                elif tile[:-1] in ("fox", "ret", "mla"):
                    branch, half = ("fox", "ret", "mla").index(tile[:-1]), int(tile[-1])
                    gate = f"gate{branch}{half}"
                    tile_act_done(layer, gate)
                    src = ps[:, bank:bank + 2, :]
                    if branch == 0:
                        i = v.tensor_tensor(merged[half][:], gates[gate_slot(gate)][:], src, ALU.mult)
                    else:
                        dve.wait_ge(tile_dve, TILES.dve[TILES.number[layer, tile]] - 1)
                        then(v.tensor_tensor(mixed[:], gates[gate_slot(gate)][:], src, ALU.mult))
                        i = v.tensor_tensor(merged[half][:], merged[half][:], mixed[:], ALU.add)
                elif tile[:-1] == "out":
                    cols = slice(512 * int(tile[-1]), 512 * (int(tile[-1]) + 1))
                    i = v.tensor_tensor(x_sb[:, :, cols], x_sb[:, :, cols], ps[:, bank:bank + 2, :], ALU.add)
                else:
                    dst, cols = token_dst(tile, 1)
                    i = v.tensor_copy(dst, ps[:, bank + 1, 0:cols])
                i.then_inc(tile_dve, 1)

            def turned_tile(layer, tile):
                bank = 2 * (TILES.number[layer, tile] % 2)
                hi, lo, weights, first, n = turn_target(layer, tile)
                if hi is None:
                    dve.wait_ge(turned_ready, turn_count(layer, tile))
                    dst, rows = plain_target(tile)
                    i = v.tensor_copy(dst[0:rows, 2:4], ps[0:rows, bank + 1].rearrange("p (c t) -> p c t", c=2))
                else:
                    tile_act_done(layer, tile)
                    for c in range(n):
                        src = ps[:, bank + c // 2, SEQ * (c % 2):SEQ * (c % 2 + 1)]
                        was = hi.bitcast(F32)[:, first + c]
                        if weights is None:
                            i = v.tensor_tensor(lo[:, first + c], src, was, ALU.subtract)
                        else:
                            i = v.scalar_tensor_tensor(lo[:, first + c], src, weights[c], was, ALU.mult, ALU.subtract)
                i.then_inc(tile_dve, 1)

            def rope(t, half, cos, sin):
                c = cos.rearrange("p (b d) -> p b d", b=NB).unsqueeze(2)
                s = sin.rearrange("p (b d) -> p b d", b=NB).unsqueeze(2)
                n = t.shape[2]
                tmp = turned[:, :, 0:n, 0:2 * half]
                v.tensor_tensor(tmp[:, :, :, 0:half], t[:, :, :, half:], s[:, :, :, 0:half].broadcast_to([P, NB, n, half]), ALU.mult)
                then(v.tensor_tensor(tmp[:, :, :, half:], t[:, :, :, 0:half], s[:, :, :, half:].broadcast_to([P, NB, n, half]), ALU.mult))
                then(v.tensor_tensor(t, t, c.broadcast_to([P, NB, n, 2 * half]), ALU.mult))
                return v.tensor_tensor(t, t, tmp, ALU.add)

            def heads_split(layer, u):
                dve.wait_ge(heads_act, 4 * layer + u + 1)
                hi, lo = (ofoxT_hi, ofoxT_lo) if u < 2 else (omlaT_hi, omlaT_lo)
                cs = slice(2 * (u % 2), 2 * (u % 2) + 2)
                v.tensor_tensor(lo[:, cs], ps[:, 4 + u % 2].rearrange("p (c t) -> p c t", c=2),
                                hi.bitcast(F32)[:, cs], ALU.subtract).then_inc(heads_dve, 1)

            def side(layer, what, k):
                if what in ("norm_mix", "norm_ffn"):
                    scales(NB)
                    for b in range(NB):
                        i = v.tensor_scalar(normed[:, b], x_sb[:, b], stat[:, 24 + b:25 + b], None, ALU.mult)
                    i.then_inc(source_ready, 1)
                elif what == "forget":
                    tile_act_done(layer, "ff")
                    dve.wait_ge(tile_dve, TILES.dve[TILES.number[layer, "ff"]])
                    v.memset(log_f[:], 0.0)
                    z, az = forget[:, 0], forget[:, 1]
                    then(v.tensor_tensor(z, z, forget_bias[:, layer].unsqueeze(1).broadcast_to([P, NB, HEADS]), ALU.add))
                    v.scalar_tensor_tensor(az, z, -1.0, z, ALU.mult, ALU.max).then_inc(logits_abs, 1)
                elif what == "latent_norm":
                    dve.wait_ge(log_terms, layer + 1)
                    v.scalar_tensor_tensor(log_f[:, :, 0:HEADS], forget[:, 0], 0.0, forget[:, 3], ALU.min,
                                           ALU.subtract).then_inc(forget_ready, 1)
                    scales(2 * NB)
                    for b in range(NB):
                        v.tensor_scalar(cq[:, b], cq[:, b], stat[:, 24 + b:25 + b], None, ALU.mult)
                    for b in range(NB):
                        i = v.tensor_scalar(ckvkr[:, b, 0:KV_RANK], ckvkr[:, b, 0:KV_RANK],
                                            stat[:, 26 + b:27 + b], None, ALU.mult)
                    i.then_inc(source_ready, 1)
                elif what == "cumulate":
                    dve.wait_ge(right_act, use_of_7(layer, "cumulate", 0) + 1)
                    v.tensor_scalar(neg_cum_T[:], cum_T[:], -1.0, None, ALU.mult).then_inc(neg_cum_ready, 1)
                elif what == "mla_rope_q":
                    tile_act_done(layer, "uq1")
                    dve.wait_ge(tile_dve, TILES.dve[TILES.number[layer, "uq1"]])
                    rope(mq[:, :, :, NOPE:], ROPE // 2, const("mla_cos"), const("mla_sin")).then_inc(source_ready, 1)
                elif what == "mla_make_k":
                    tile_act_done(layer, "uk")
                    kr = ckvkr[:, :, KV_RANK:].unsqueeze(2)
                    then(rope(kr, ROPE // 2, const("mla_cos"), const("mla_sin")))
                    v.tensor_copy(mk[:, :, :, NOPE:], kr.broadcast_to([P, NB, HEADS, ROPE])).then_inc(source_ready, 1)
                elif what in ("ret_rope_q", "ret_rope_k"):
                    t = rq if what[-1] == "q" else rk
                    tile_act_done(layer, "r" + what[-1])
                    dve.wait_ge(tile_dve, TILES.dve[TILES.number[layer, "r" + what[-1]]])
                    rope(t[:], RET_K // 2, const("ret_cos"), const("ret_sin")).then_inc(source_ready, 1)
                elif what == "softmax":
                    if k < 16:
                        n = 16 * layer + k
                        use = use_of_6(layer, "softmax", k)
                        dve.wait_ge(scores_ready, use + 1)
                        scale = 1.0 if k < HEADS else QK ** -0.5
                        mx = 30 + 2 * (k % 2)
                        for b in range(NB):
                            cols = slice(P * b, P * b + P * (b + 1))
                            i = v.tensor_tensor_reduce(
                                out=prob[:, k % 2, cols], in0=ps[:, 6, cols], in1=causal[:, P * (1 - b):],
                                scale=scale, scalar=-3e38, op0=ALU.add, op1=ALU.max, accum_out=stat[:, mx + b:mx + b + 1])
                        i.then_inc(scores_taken, 1)
                        dve.wait_ge(scores_taken, use + 1)
                        at_neg = 34 + 2 * (k % 2)
                        v.tensor_scalar(stat[:, at_neg:at_neg + 2], stat[:, mx:mx + 2], -1.0, None,
                                        ALU.mult).then_inc(row_max_ready, 1)
                    if k < 16:
                        dve.wait_ge(prob_exp, 16 * layer + k + 1)
                        sums = 38 + 2 * (k % 2)
                        inv = 46 + 2 * (k % 2)
                        then(v.reciprocal(stat[:, inv:inv + 2], stat[:, sums:sums + 2]))
                        for b in range(NB):
                            cols = slice(P * b, P * b + P * (b + 1))
                            i = v.tensor_scalar(prob[:, k % 2, cols], prob[:, k % 2, cols],
                                                stat[:, inv + b:inv + b + 1], None, ALU.mult)
                        i.then_inc(prob_ready, 1)
                    if k >= 2 and (k - 2) % 4 == 3:
                        heads_split(layer, (k - 2) // 4)
                elif what == "retention":
                    if k < HEADS:
                        use = use_of_6(layer, "retention", k)
                        dve.wait_ge(scores_ready, use + 1)
                        v.tensor_tensor(prob_T[:, k % 2, 0:SEQ], ps[:, 6, 0:SEQ], decay[:, k], ALU.mult)
                        i = v.tensor_tensor(prob_T[:, k % 2, SEQ:], ps[:, 6, SEQ:SEQ + P], decay[:, k, 0:P], ALU.mult)
                        i.then_inc(scores_taken, 1)
                    if k:
                        r = k - 1
                        dve.wait_ge(right_act, use_of_7(layer, "retention", r) + 1)
                        for b in range(NB):
                            i = v.bn_stats(bn[:, r, b], o_ret[:, b, RET_V * r:RET_V * k])
                        then(i)
                        for b in range(NB):
                            i = v.bn_aggr(ret_stat[:, b, r], bn[:, r, b])
                        i.then_inc(ret_var_ready, 1)
                elif what == "ret_norm":
                    dve.wait_ge(ret_dev_ready, layer + 1)
                    then(v.reciprocal(ret_dev[:], ret_dev[:]))
                    for b in range(NB):
                        for r in range(HEADS):
                            cols = slice(RET_V * r, RET_V * (r + 1))
                            i = v.tensor_scalar(o_ret[:, b, cols], o_ret[:, b, cols], ret_stat[:, b, r, 0:1],
                                                ret_dev[:, b, r:r + 1], ALU.subtract, ALU.mult)
                    then(i)
                    tile_act_done(layer, "rg1")
                    v.tensor_tensor(o_ret[:], o_ret[:], rg[:], ALU.mult).then_inc(source_ready, 1)

            def mixer(layer):
                g = G_MIX[layer]
                if layer == 0:
                    for first in range(AHEAD):
                        split(first)
                for step in PLAN:
                    if step[0] == "granule":
                        if g + AHEAD < G_MOE:
                            split(g + AHEAD)
                        if step[3]:
                            take(layer, step[1], g)
                        g += 1
                    elif step[0] == "turn":
                        turned_tile(layer, step[1])
                    else:
                        side(layer, *step[1:])

            v.memset(eps_col[:], EPS)
            v.memset(stat[:], 0.0)
            v.memset(zeros[:], 0.0).then_inc(zeroed, 1)
            dve.wait_ge(zeroed, 1)
            dve.wait_ge(router_hi_ready, 1)
            v.tensor_tensor(router_lo[:], router_raw[:], router_hi.bitcast(F32)[:], ALU.subtract).then_inc(router_lo_ready, 1)
            mixer(0)

            dve.sem_inc(d_act_ready, 2)
            with dve.Fori(0, N_DENSE_TURNS) as turn_no:
                def multiply(i):
                    dve.wait_ge(granule_used, turn_no * DENSE_STEP + (G_DENSE + 2 * i + 2))
                    dve.wait_ge(d_silu_ready, turn_no * 2 + (i + 1))
                    v.tensor_tensor(d_act[:, i], d_silu[:, i], ps[:, 2 * i + 1, :], ALU.mult).then_inc(d_act_ready, 1)

                def lo_part(i):
                    dve.wait_ge(d_hi_ready, turn_no * 2 + (i + 1))
                    v.tensor_tensor(d_act_lo[:, i], d_act[:, i], d_act_hi.bitcast(F32)[:, i], ALU.subtract).then_inc(d_lo_ready, 1)

                for p in range(DENSE_STEP):
                    split(G_DENSE + p + AHEAD, turn_no, 1, DENSE_STEP)
                    if p == 1:
                        multiply(0)
                    if p == 2:
                        lo_part(0)
                    if p == 3:
                        multiply(1)
                    if p == 4:
                        lo_part(1)
            dve.wait_ge(d_summed, 1)
            v.tensor_tensor(x_sb[:].rearrange("p b (n c) -> p (b n) c", n=2),
                            x_sb[:].rearrange("p b (n c) -> p (b n) c", n=2), ps[:, 4:8, :], ALU.add).then_inc(x_summed, 1)
            dve.wait_ge(x_summed, 1)
            mixer(1)

            dve.wait_ge(rows_in, 16)
            dve.wait_ge(turned_ready, turn_count(1, "ffn1"))
            v.tensor_tensor(normed[:], normed[:], ffn_w_row[:].unsqueeze(1).broadcast_to([P, NB, D]),
                            ALU.mult).then_inc(h_wide_ready, 1)
            dve.wait_ge(h_hi_ready, 1)
            v.tensor_tensor(h_lo[:], normed[:], h_hi.bitcast(F32)[:], ALU.subtract).then_inc(h_lo_ready, 1)

            logits = rt[:, LOGITS]
            dve.wait_ge(logits_ready, 1)
            then(v.tensor_copy(logits, ps[:, 4, 0:NB * N_EXPERTS].rearrange("p (b e) -> p b e", b=NB)))
            then(v.tensor_reduce(stat[:, 42:44], logits, AX.X, ALU.max))
            v.tensor_scalar(stat[:, 44:46], stat[:, 42:44], -1.0, None, ALU.mult).then_inc(logit_max_ready, 1)
            full = [P, NB, N_EXPERTS, N_EXPERTS]
            other = logits.unsqueeze(2).broadcast_to(full)
            this = logits.unsqueeze(3).broadcast_to(full)
            before = const("before").rearrange("p (i j) -> p i j", i=N_EXPERTS)
            v.tensor_tensor(pairs[:, 0], other, this, ALU.is_gt)
            then(v.tensor_tensor(pairs[:, 1], other, this, ALU.is_equal))
            then(v.tensor_tensor(pairs[:, 1], pairs[:, 1], before.unsqueeze(1).broadcast_to(full), ALU.mult))
            then(v.tensor_tensor(pairs[:, 0], pairs[:, 0], pairs[:, 1], ALU.add))
            then(v.tensor_reduce(rt[:, BEATEN], pairs[:, 0], AX.X, ALU.add))
            v.tensor_scalar(rt[:, CHOSEN], rt[:, BEATEN], 1.5, None, ALU.is_lt).then_inc(chosen_ready, 1)
            dve.wait_ge(chosen_ready, 1)
            dve.wait_ge(logit_exp, 1)
            then(v.tensor_tensor(rt[:, WEIGHTS], rt[:, EXPS], rt[:, CHOSEN], ALU.mult))
            then(v.tensor_reduce(stat[:, 52:54], rt[:, WEIGHTS], AX.X, ALU.add))
            then(v.reciprocal(stat[:, 54:56], stat[:, 52:54]))
            then(v.tensor_tensor(rt[:, WEIGHTS], rt[:, WEIGHTS],
                                 stat[:, 54:56].unsqueeze(2).broadcast_to([P, NB, N_EXPERTS]), ALU.mult))
            dve.wait_ge(ranks_ready, 1)
            then(v.tensor_tensor(rt[:, RANKS], rt[:, CHOSEN],
                                 ps[:, 5, 0:NB * N_EXPERTS].rearrange("p (b e) -> p b e", b=NB), ALU.mult))
            for half in range(2):
                dst = route[:, N_EXPERTS * half:N_EXPERTS * (half + 1)]
                v.tensor_scalar(dst[:, :, 0:2], rt[:, RANKS].rearrange("p b e -> p e b"), -1.0 - P * half, None, ALU.add)
                v.tensor_copy(dst[:, :, 2:4], rt[:, WEIGHTS].rearrange("p b e -> p e b"))
            then(v.tensor_reduce(stat[:, 56:57], ps[:, 5, 2 * N_EXPERTS:3 * N_EXPERTS], AX.X, ALU.max))
            v.tensor_copy(most[:], stat[:, 56:57]).then_inc(route_ready, 1)
            dve.wait_ge(route_ready, 1)

            def expert(e, E):
                dve.wait_ge(misc_dve, E * MISC_DVE + 1)
                v.tensor_copy(here[:].unsqueeze(1), route[:, bass.ds(E, 1), :]).then_inc(here_ready, 1)
                dve.wait_ge(here_ready, E + 1)
                for b in range(NB):
                    i = v.tensor_scalar(onehot[:, b], iota, here[:, b:b + 1], None, ALU.is_equal)
                i.then_inc(onehot_ready, 1)
                for p in range(AHEAD):
                    split(G_MOE + p, E, EXPERT_G // FFN_RING, EXPERT_G)
                dve.wait_ge(gathered, E + 1)
                v.tensor_copy(xg_lo[:].rearrange("p (a k) t -> p a (k t)", a=2), ps[:, 2:4, :]).then_inc(xg_lo_ready, 1)

                def turned_lo(i):
                    dve.wait_ge(misc_act, E * MISC_ACT + (1 + i + 2))
                    v.tensor_tensor(e_actT_lo[:, i % 2].rearrange("p a b -> p (a b)"), ps[:, 6 + (i + 1) % 2, :],
                                    e_actT_hi.bitcast(F32)[:, i % 2].rearrange("p a b -> p (a b)"),
                                    ALU.subtract).then_inc(misc_dve, 1)

                for p, (what, i, half) in enumerate(EXPERT_ORDER):
                    if p + AHEAD < EXPERT_G:
                        split(G_MOE + p + AHEAD, E, EXPERT_G // FFN_RING, EXPERT_G)
                    if what == "gate" and half == 1 and i >= 1:
                        turned_lo(i - 1)
                    if what == "up" and half == 1:
                        dve.wait_ge(granule_used, E * EXPERT_G + (G_MOE + p + 1))
                        dve.wait_ge(e_silu_ready, E * N_FT + (i + 1))
                        v.tensor_tensor(e_act[:, i % 2], e_silu[:, i % 2], ps[:, 2 * (i % 2) + 1, :],
                                        ALU.mult).then_inc(e_act_ready, 1)
                    if what == "down" and half == 1 and i == N_FT - 2:
                        turned_lo(N_FT - 1)
                dve.wait_ge(y_hi_ready, E + 1)
                v.tensor_tensor(y_lo[:].rearrange("p (a c) -> p a c", a=2), ps[:, 4:6, :],
                                y_hi.bitcast(F32)[:].rearrange("p (a c) -> p a c", a=2),
                                ALU.subtract).then_inc(y_lo_ready, 1)
                for b in range(NB):
                    for n in range(2):
                        u = 2 * b + n
                        dve.wait_ge(misc_ready, E * MISC_USES + (9 + u))
                        cols = slice(512 * n, 512 * (n + 1))
                        v.scalar_tensor_tensor(x_sb[:, b, cols], ps[:, 6 + u % 2, :], here[:, 2 + b:3 + b],
                                               x_sb[:, b, cols], ALU.mult, ALU.add).then_inc(misc_dve, 1)

            dve.sem_inc(misc_dve, 1)
            with dve.Fori(0, N_EXPERTS) as e:
                expert(e, e)
            dve.wait_ge(misc_dve, N_EXPERTS * MISC_DVE + 1)
            many = dve.value_load(most[0:1, 0:1], min_val=0, max_val=SEQ)
            with dve.If(many > P):
                with dve.Fori(0, N_EXPERTS) as e:
                    expert(e, e + N_EXPERTS)
                dve.wait_ge(misc_dve, 2 * N_EXPERTS * MISC_DVE + 1)
            dve.sem_inc(final_in, 1)
            dve.wait_ge(rows_in, 32)
            scales(NB)
            for b in range(NB):
                i = v.scalar_tensor_tensor(result[:, b], x_sb[:, b], stat[:, 24 + b:25 + b], final_row[:],
                                           ALU.mult, ALU.mult)
            i.then_inc(final_in, 1)


_INS = ["x", "norm_mix_w", "w_in", "fox_f_bias", "ret_gn_w", "mla_q_norm_w", "mla_kv_norm_w", "mla_w_uq",
        "mla_w_uk", "mla_w_uv", "w_br_fox", "w_br_ret", "w_br_mla", "w_out", "norm_ffn_w", "dense_w_gate",
        "dense_w_up", "dense_w_down", "moe_w_router", "moe_w_gate", "moe_w_up", "moe_w_down", "final_norm_w"]


def kernel(**inputs):
    import numpy as _np
    import concourse.bacc as _bacc
    from concourse import mybir as _mybir
    from concourse.bass_utils import run_bass_kernel_spmd as _run

    nc = _bacc.Bacc("TRN2", target_bir_lowering=False, num_devices=1)
    arrays, args = {}, []
    for name in _INS:
        a = _np.ascontiguousarray(inputs[name])
        arrays[f"in_{name}_dram"] = a
        args.append(nc.dram_tensor(f"in_{name}_dram", a.shape, _mybir.dt.from_np(a.dtype), kind="ExternalInput").ap())
    table = shape_constants()
    arrays["in_consts_dram"] = table
    args.append(nc.dram_tensor("in_consts_dram", table.shape, _mybir.dt.float32, kind="ExternalInput").ap())
    out = nc.dram_tensor("out_0_dram", (1, SEQ, D), _mybir.dt.float32, kind="ExternalOutput").ap()
    build(nc, *args, out)
    r = _run(nc, [arrays], core_ids=[0])
    return r.results[0]["out_0_dram"]
```

```python
from contextlib import ExitStack

import numpy as np
import concourse.bass as bass
from concourse import mybir

F32 = mybir.dt.float32
F32R = mybir.dt.float32r
I32 = mybir.dt.int32
ALU = mybir.AluOpType
ACT = mybir.ActivationFunctionType
AX = mybir.AxisListType

P = 128
D = 1024
SEQ = 256
DEPTH = 2
HEADS = 8
FOX_D = 64
RET_K, RET_V = 64, 128
Q_RANK, KV_RANK = 384, 256
NOPE, ROPE = 64, 32
QK = NOPE + ROPE
D_FF = 3584
N_EXPERTS = 8
EPS = 1e-6
THETA = 10000.0
NB = SEQ // P
KC = D // P
MASKED = -1e30

WIDTHS = dict(fq=512, fk=512, fv=512, ff=8, rq=512, rk=512, rv=1024, rg=1024,
              cq=Q_RANK, ckv=KV_RANK, kr=ROPE, gl=3 * D)
START = {}
_at = 0
for _name, _w in WIDTHS.items():
    START[_name] = _at
    _at += _w
D_IN = _at

CONST_PARTS = dict(ident=P, causal=2 * P, cum=2 * P, decay=HEADS * 2 * P, ret_cos=NB * RET_K,
                   ret_sin=NB * RET_K, mla_cos=NB * ROPE, mla_sin=NB * ROPE, iota=P,
                   before=N_EXPERTS * N_EXPERTS)
CONST_AT = {}
_at = 0
for _name, _w in CONST_PARTS.items():
    CONST_AT[_name] = _at
    _at += _w
N_CONST = _at
FIRST_CONST = CONST_AT["decay"]

N_PARAM = 2 * DEPTH * KC + DEPTH * KC + DEPTH * (Q_RANK + KV_RANK) // P
PARAM_AT = dict(mix=0, ffn=DEPTH * KC, gn=2 * DEPTH * KC, qn=3 * DEPTH * KC,
                kvn=3 * DEPTH * KC + DEPTH * Q_RANK // P)


def shape_constants():
    c = np.zeros((P, N_CONST), np.float32)

    def put(name, a):
        c[:, CONST_AT[name]:CONST_AT[name] + CONST_PARTS[name]] = a.reshape(P, -1)

    i = np.arange(P)
    put("ident", np.eye(P, dtype=np.float32))
    put("causal", np.concatenate([np.zeros((P, P)), np.where(i[None] <= i[:, None], 0.0, MASKED)], 1))
    put("cum", (i[:, None] <= np.arange(2 * P)[None]).astype(np.float32))
    gamma = 1.0 - 2.0 ** (-5.0 - np.arange(HEADS, dtype=np.float64))
    gap = np.arange(2 * P)[None] - i[:, None]
    decay = np.where(gap[:, None] >= 0, np.exp(np.maximum(gap, 0)[:, None] * np.log(gamma)[None, :, None]), 0.0)
    put("decay", decay * RET_K ** -0.5)
    for name, d in (("ret", RET_K), ("mla", ROPE)):
        inv = np.float32(THETA) ** (-np.arange(0, d, 2, dtype=np.float32) / np.float32(d))
        ang = (np.arange(SEQ, dtype=np.float32)[:, None] * inv.astype(np.float32)[None]).astype(np.float32)
        cos, sin = np.cos(ang), np.sin(ang)
        put(name + "_cos", np.concatenate([cos, cos], 1).reshape(NB, P, d).transpose(1, 0, 2))
        put(name + "_sin", np.concatenate([-sin, sin], 1).reshape(NB, P, d).transpose(1, 0, 2))
    put("iota", np.broadcast_to(i[None], (P, P)))
    e = np.arange(N_EXPERTS)
    put("before", np.broadcast_to((e[None, :] < e[:, None]).astype(np.float32), (P, N_EXPERTS, N_EXPERTS)))
    return c


GCOLS = 2048
MIX_RING = 4
DENSE_RING = 6
EXPERT_RING = 7
PAIR_RING = 3
AHEAD = 2
FT = 512
N_FT = D_FF // FT
DENSE_STEP = 6
N_DENSE_TURNS = D_FF // 256 // 2
EXPERT_G = 6 * N_FT


def mixer_plan():
    steps = []

    def project(tile, n, sides=()):
        sides = list(sides)
        for j in range(n):
            steps.append(("granule", tile, j, j == n - 1))
            if sides:
                for s in sides.pop(0):
                    steps.append(("side",) + s)

    def side(what, k=0):
        steps.append(("side", what, k))

    def turn(tile):
        steps.append(("turn", tile))

    side("norm_mix")
    turn("norm0")
    turn("norm1")
    project("fq", 2)
    project("ff", 1)
    project("cq", 2)
    project("ckvkr", 2)
    side("forget")
    project("fk", 2)
    side("latent_norm")
    project("fv", 2)
    side("cumulate")
    turn("cqT")
    turn("ckvT")
    sm = lambda k: ("softmax", k)
    project("uq0", 1, [[sm(0)]])
    project("uq1", 1, [[sm(1)]])
    side("mla_rope_q")
    project("uk", 1, [[sm(2)]])
    side("mla_make_k")
    project("uv", 1, [[sm(3)]])
    project("rq", 2, [[sm(4)], [sm(5)]])
    side("ret_rope_q")
    project("rk", 2, [[sm(6)], [sm(7)]])
    for t in ("mqT0", "mqT1", "mkT0", "mkT1"):
        turn(t)
    side("ret_rope_k")
    project("rv0", 2, [[sm(8)], [sm(9)]])
    project("rv1", 2, [[sm(10)], [sm(11)]])
    turn("rqT")
    project("rg0", 2, [[sm(12)], [sm(13)]])
    turn("rkT")
    project("rg1", 2, [[sm(14)], [sm(15)]])
    ret = lambda k: ("retention", k)
    project("gate00", 2, [[sm(16), ret(0)], [sm(17), ret(1)]])
    project("gate10", 2, [[ret(2)], [ret(3)]])
    project("gate20", 2, [[ret(4)], [ret(5)]])
    project("fox0", 1, [[ret(6)]])
    project("mla0", 1, [[ret(7)]])
    project("gate01", 2, [[ret(8)], [("ret_norm", 0)]])
    project("gate11", 2)
    project("gate21", 2)
    turn("oretT0")
    project("fox1", 1)
    turn("oretT1")
    project("mla1", 1)
    project("ret0", 2)
    steps.append(("granule", "ret1", 0, False))
    turn("mergedT0")
    steps.append(("granule", "ret1", 1, True))
    steps.append(("granule", "out0", 0, False))
    turn("mergedT1")
    steps.append(("granule", "out1", 0, False))
    steps.append(("granule", "out0", 1, True))
    steps.append(("granule", "out1", 1, True))
    side("norm_ffn")
    turn("ffn0")
    turn("ffn1")
    return steps


PLAN = mixer_plan()

TAKEN_BY_ACT_ALONE = ("rg0", "rg1", "gate")
TAKEN_BY_DVE_ALONE = ("fox", "ret", "mla", "out")


def takers(tile):
    if tile.startswith(TAKEN_BY_ACT_ALONE):
        return 1, 0
    if tile[:-1] in TAKEN_BY_DVE_ALONE:
        return 0, 1
    return 1, 1


class Tiles:

    def __init__(self):
        self.bank, self.before, self.act, self.dve = {}, {}, {}, {}
        last, alternate, a, d = {}, 0, 0, 0
        for layer in range(DEPTH):
            for step in PLAN:
                if step[0] == "side":
                    continue
                key = layer, step[1]
                if step[0] == "turn" or step[2] == 0:
                    if step[1] in ("mergedT0", "mergedT1"):
                        self.bank[key], self.before[key] = 4 + 2 * int(step[1][-1]), None
                    else:
                        bank = 2 * (alternate % 2)
                        alternate += 1
                        self.bank[key], self.before[key] = bank, last.get(bank)
                        last[bank] = key
                if step[0] == "turn" or step[3]:
                    by_act, by_dve = takers(step[1])
                    a, d = a + by_act, d + by_dve
                    self.act[key], self.dve[key] = a, d


TILES = Tiles()


def numbered(keys_of):
    number = {}
    for layer in range(DEPTH):
        for step in PLAN:
            for key in keys_of(step):
                number[(layer,) + key] = len(number)
    return number


def scores_in(step):
    if step[0] == "side" and (step[1], step[2] < (16 if step[1] == "softmax" else HEADS)) in (
            ("softmax", True), ("retention", True)):
        yield step[1:]


def right_in(step):
    if step[1] == "cumulate":
        yield "cumulate", 0
    elif step[1] == "softmax" and 1 <= step[2] < 17 or step[1] == "retention" and step[2]:
        yield step[1], step[2] - 1


USE_OF_6 = numbered(scores_in)
USE_OF_7 = numbered(right_in)
TURNS = numbered(lambda step: [step[1:]] if step[0] == "turn" else [])
WIDE_SPLITS = numbered(lambda step: [step[1:]] if step[0] == "turn" and step[1][:-1] in (
    "norm", "ffn", "oretT", "mergedT") else [])


def use_of_6(layer, what, k):
    return USE_OF_6[layer, what, k]


def use_of_7(layer, what, k):
    return USE_OF_7[layer, what, k]


def turn_count(layer, tile):
    return TURNS[layer, tile] + 1


def gate_slot(tile):
    branch, half = int(tile[4]), int(tile[5])
    return (branch + 3 * half) % 5


N_PARTS = 4
MISC_USES = N_PARTS + 1 + N_FT
MISC_ACT = 1 + N_FT
MISC_DVE = N_PARTS + N_FT


def misc_taken(u, E, half):
    a = max(u - N_PARTS + 1, 0)
    d = u + 1 if u < N_PARTS else u
    return E * MISC_ACT + (1 + a), E * MISC_DVE + (1 + max(d, 0) + N_PARTS * half)


LOGITS, EXPS, BEATEN, WEIGHTS, RANKS = range(5)
MIX_G = sum(s[0] == "granule" for s in PLAN)
G_MIX = [0, MIX_G + N_DENSE_TURNS * DENSE_STEP]
G_DENSE = MIX_G
G_MOE = G_MIX[1] + MIX_G
N_GRANULES = G_MOE + 2 * N_EXPERTS * EXPERT_G


class Stream:

    def __init__(self):
        self.slot, self.loads, self.before = [], [], []
        loads, last = [0] * EXPERT_RING, [None] * EXPERT_RING
        for g in range(N_GRANULES):
            if g < G_DENSE:
                s = g % MIX_RING
            elif g < G_MIX[1]:
                s = (g - G_DENSE) % DENSE_RING
            elif g < G_MOE:
                s = (g - G_MIX[1]) % MIX_RING
            else:
                s = (g - G_MOE) % EXPERT_RING
            loads[s] += 1
            self.slot.append(s)
            self.loads.append(loads[s])
            self.before.append(last[s])
            last[s] = g


STREAM = Stream()


def expert_order():
    order = []
    for i in range(N_FT + 1):
        if i < N_FT:
            order += [("gate", i, 0), ("gate", i, 1), ("up", i, 0), ("up", i, 1)]
        if i > 0:
            order += [("down", i - 1, 0), ("down", i - 1, 1)]
    return order


EXPERT_ORDER = expert_order()


def build(nc, x, norm_mix_w, w_in, fox_f_bias, ret_gn_w, mla_q_norm_w, mla_kv_norm_w, mla_w_uq,
          mla_w_uk, mla_w_uv, w_br_fox, w_br_ret, w_br_mla, w_out, norm_ffn_w, dense_w_gate,
          dense_w_up, dense_w_down, moe_w_router, moe_w_gate, moe_w_up, moe_w_down, final_norm_w,
          consts, out):
    ctx = ExitStack()

    def sb(name, shape, dtype=F32):
        return ctx.enter_context(nc.sbuf_tensor(name, shape, dtype))

    def sem(name):
        return ctx.enter_context(nc.semaphore(name))

    with ctx:
        x_sb = sb("x_sb", [P, NB, D])
        cst = sb("cst", [P, N_CONST])
        param_T = sb("param_T", [P, N_PARAM])
        hT_hi = sb("hT_hi", [P, KC, SEQ], F32R)
        hT_lo = sb("hT_lo", [P, KC, SEQ], F32R)
        raw_low = sb("raw_low", [P, MIX_RING, GCOLS])
        w_hi = sb("w_hi", [P, PAIR_RING, GCOLS], F32R)
        w_lo = sb("w_lo", [P, PAIR_RING, GCOLS], F32R)
        pick_head = sb("pick_head", [P, HEADS], F32R)
        forget_bias = sb("forget_bias", [P, DEPTH, HEADS])
        router_raw = sb("router_raw", [P, KC, N_EXPERTS])
        router_w = sb("router_w", [P, KC, 2, N_EXPERTS], F32R)
        cum_01 = sb("cum_01", [P, 2 * P], F32R)
        stat = sb("stat", [P, 64])
        eps_col = sb("eps_col", [P, 1])
        zeros = sb("zeros", [P, P], F32R)
        table_loaded = sb("table_loaded", [P, 1])
        ARENA = 83 * 1024
        arena = sb("arena", [P, ARENA // 4])
        base = nc.sbuf_base - ARENA
        used = {}

        def at(region, offset, name, shape, dtype=F32):
            size = 4 * int(np.prod(shape[1:]))
            used[region] = max(used.get(region, 0), offset + size)
            start = dict(A=0, B=16384, C=28672, D=40960, R=57344, E=65536, X=0)[region]
            assert start + offset + size <= ARENA, (name, start + offset + size)
            return nc.alloc_sbuf_tensor_at(name, shape, dtype, offset=base + start + offset)

        K = 1024
        normed = at("A", 0, "normed", [P, NB, D])
        cq = at("A", 0, "cq", [P, NB, Q_RANK])
        ckvkr = at("A", 3 * K, "ckvkr", [P, NB, KV_RANK + ROPE])
        cqT_hi = at("A", 5632, "cqT_hi", [P, Q_RANK // P, SEQ], F32R)
        cqT_lo = at("A", 5632 + 3 * K, "cqT_lo", [P, Q_RANK // P, SEQ], F32R)
        ckvT_hi = at("A", 5632 + 6 * K, "ckvT_hi", [P, KV_RANK // P, SEQ], F32R)
        ckvT_lo = at("A", 5632 + 8 * K, "ckvT_lo", [P, KV_RANK // P, SEQ], F32R)
        omlaT_hi = at("A", 0, "omlaT_hi", [P, 4, SEQ], F32R)
        omlaT_lo = at("A", 4 * K, "omlaT_lo", [P, 4, SEQ], F32R)
        mergedT_hi = at("A", 0, "mergedT_hi", [P, KC, SEQ], F32R)
        mergedT_lo = at("A", 8 * K, "mergedT_lo", [P, KC, SEQ], F32R)
        mv = at("A", 12 * K, "mv", [P, NB, 512])
        o_ret = at("A", 8 * K, "o_ret", [P, NB, D])
        fqT = at("B", 0, "fqT", [P, 4, SEQ])
        fkT = at("B", 4 * K, "fkT", [P, 4, SEQ])
        fv = at("B", 8 * K, "fv", [P, NB, 512])
        rg = at("B", 0, "rg", [P, NB, D])
        mq = at("C", 0, "mq", [P, NB, HEADS, QK])
        mk = at("C", 6 * K, "mk", [P, NB, HEADS, QK])
        rv = at("C", 0, "rv", [P, NB, D])
        merged = [at("B", 8 * K, "merged0", [P, NB, 512]), at("C", 8 * K, "merged1", [P, NB, 512])]
        mqT = at("D", 0, "mqT", [P, HEADS, SEQ])
        mkT = at("D", 8 * K, "mkT", [P, HEADS, SEQ])
        gates = [at("D", 4 * K * i, f"gates{i}", [P, NB, 512]) for i in range(4)]
        gates.append(at("R", 4 * K, "gates4", [P, NB, 512]))
        turned = at("E", 0, "turned", [P, NB, HEADS, RET_K])
        log_f = at("D", 4 * K, "log_f", [P, NB, P])
        cum_hi, cum_lo, neg_hi, neg_lo = (at("D", (5 + i) * K, n, [P, SEQ], F32R) for i, n in enumerate(
            ("cum_hi", "cum_lo", "neg_hi", "neg_lo")))
        latent_scratch = at("C", 0, "latent_scratch", [P, 2 * NB, Q_RANK])
        params = at("C", 0, "params", [N_PARAM, P])
        rq = at("R", 0, "rq", [P, NB, HEADS, RET_K])
        rk = at("R", 4 * K, "rk", [P, NB, HEADS, RET_K])
        mixed = at("R", 0, "mixed", [P, NB, 512])
        rqT = at("E", 0, "rqT", [P, 4, SEQ])
        rkT = at("E", 4 * K, "rkT", [P, 4, SEQ])
        ofoxT_hi = at("E", 8 * K, "ofoxT_hi", [P, 4, SEQ], F32R)
        ofoxT_lo = at("E", 12 * K, "ofoxT_lo", [P, 4, SEQ], F32R)
        prob = at("E", 16 * K, "prob", [P, 2, 384])
        forget = sb("forget", [P, 4, NB, HEADS])
        bn = sb("bn", [P, HEADS, NB, 6])
        ret_stat = sb("ret_stat", [P, NB, HEADS, 2])
        ret_dev = sb("ret_dev", [P, NB, HEADS])
        prob_T = sb("prob_T", [P, 2, 384])
        raw_high = at("X", ARENA - 4 * GCOLS * 2, "raw_high", [P, DENSE_RING - MIX_RING, GCOLS])
        d_silu = at("X", 0, "d_silu", [P, 2, 512])
        d_act = at("X", 4 * K, "d_act", [P, 2, 512])
        d_act_hi = at("X", 8 * K, "d_act_hi", [P, 2, 512], F32R)
        d_act_lo = at("X", 12 * K, "d_act_lo", [P, 2, 512], F32R)
        h_hi = at("X", 8 * K, "h_hi", [P, NB, D], F32R)
        h_lo = at("X", 16 * K, "h_lo", [P, NB, D], F32R)
        chosen_01 = at("X", 24 * K, "chosen_01", [P, NB, N_EXPERTS], F32R)
        logits_T = at("X", 25 * K, "logits_T", [2 * N_EXPERTS, SEQ])
        route = sb("route", [P, 2 * N_EXPERTS + 1, 4])
        onehot = at("X", 28 * K, "onehot", [P, NB, P], F32R)
        onehot_T = at("X", 29 * K, "onehot_T", [P, SEQ], F32R)
        xg_hi = at("X", 30 * K, "xg_hi", [P, KC, P], F32R)
        xg_lo = at("X", 34 * K, "xg_lo", [P, KC, P], F32R)
        e_silu = at("X", 38 * K, "e_silu", [P, 2, FT])
        e_act = at("X", 42 * K, "e_act", [P, 2, FT])
        e_actT_hi = at("X", 46 * K, "e_actT_hi", [P, 2, 4, P], F32R)
        e_actT_lo = at("X", 50 * K, "e_actT_lo", [P, 2, 4, P], F32R)
        y_hi = at("X", 54 * K, "y_hi", [P, D], F32R)
        y_lo = at("X", 58 * K, "y_lo", [P, D], F32R)
        assert 62 * K <= ARENA - 4 * GCOLS * 2
        rt = at("X", 46 * K, "rt", [P, 5, NB, N_EXPERTS])
        pairs = at("X", 50 * K, "pairs", [P, 2, NB, N_EXPERTS, N_EXPERTS])
        final_row = at("X", 0, "final_row", [P, D])
        result = at("X", 8 * K, "result", [P, NB, D])
        final_scratch = at("X", 16 * K, "final_scratch", [P, NB, D])
        ranks_next = sb("ranks_next", [P, NB])
        weights_here = sb("weights_here", [P, NB])
        most = sb("most", [P, 1], I32)
        ps = ctx.enter_context(nc.psum_tensor("ps", [P, 8, 512], F32))

        consts_in, tables_in, params_in, small_in, x_in, final_row_in, final_in = (sem(n) for n in (
            "consts_in", "tables_in", "params_in", "small_in", "x_in", "final_row_in", "final_in"))
        raw_in = [sem(f"raw_in{i}") for i in range(EXPERT_RING)]
        hi_split, lo_split = sem("hi_split"), sem("lo_split")
        granule_used = sem("granule_used")
        act_step, dve_step = sem("act_step"), sem("dve_step")
        params_turned, params_ready = sem("params_turned"), sem("params_ready")
        zeroed = sem("zeroed")
        router_hi_ready, router_lo_ready = sem("router_hi_ready"), sem("router_lo_ready")
        tile_act, tile_dve = sem("tile_act"), sem("tile_dve")
        turned_ready = sem("turned_ready")
        source_ready = sem("source_ready")
        first_bank_hi = sem("first_bank_hi")
        inverse_ready = sem("inverse_ready")
        squares_dve, normed_act = sem("squares_dve"), sem("normed_act")
        deviation = sem("deviation")
        logits_abs, log_terms, forget_ready = sem("logits_abs"), sem("log_terms"), sem("forget_ready")
        scores_ready, scores_taken = sem("scores_ready"), sem("scores_taken")
        row_max_ready, prob_exp, prob_ready = sem("row_max_ready"), sem("prob_exp"), sem("prob_ready")
        right_ready, right_act, neg_cum_ready = sem("right_ready"), sem("right_act"), sem("neg_cum_ready")
        heads_ready, heads_act, heads_dve = sem("heads_ready"), sem("heads_act"), sem("heads_dve")
        x_summed, final_sq = sem("x_summed"), sem("final_sq")
        ranks_copied, weights_copied = sem("ranks_copied"), sem("weights_copied")
        ret_var_ready, ret_dev_ready = sem("ret_var_ready"), sem("ret_dev_ready")
        h_hi_ready, h_lo_ready = sem("h_hi_ready"), sem("h_lo_ready")
        d_opened, d_silu_ready, d_act_ready = sem("d_opened"), sem("d_silu_ready"), sem("d_act_ready")
        d_hi_ready, d_lo_ready, d_summed = sem("d_hi_ready"), sem("d_lo_ready"), sem("d_summed")
        logits_copied, logits_turned, counts_ready = sem("logits_copied"), sem("logits_turned"), sem("counts_ready")
        logits_ready, logit_max_ready, logit_exp = sem("logits_ready"), sem("logit_max_ready"), sem("logit_exp")
        chosen_ready, ranks_ready, route_ready = sem("chosen_ready"), sem("ranks_ready"), sem("route_ready")
        onehot_ready, gathered, xg_hi_ready, xg_lo_ready = (sem(n) for n in (
            "onehot_ready", "gathered", "xg_hi_ready", "xg_lo_ready"))
        e_silu_ready, e_act_ready = sem("e_silu_ready"), sem("e_act_ready")
        misc_ready, misc_act, misc_dve = sem("misc_ready"), sem("misc_act"), sem("misc_dve")
        y_hi_ready, y_lo_ready = sem("y_hi_ready"), sem("y_lo_ready")
        final_done = [sem(f"final_done{b}") for b in range(NB)]
        stored = sem("stored")

        def const(name, *dims):
            v = cst[:, CONST_AT[name]:CONST_AT[name] + CONST_PARTS[name]]
            if len(dims) == 1:
                v = v.rearrange("p (a b) -> p a b", a=dims[0])
            return v

        ident = const("ident")
        causal = const("causal")
        cum = const("cum")
        decay = const("decay", HEADS)
        iota = const("iota")

        def channel_weights(what, layer, n):
            first = PARAM_AT[what] + layer * n
            return [param_T[:, first + c:first + c + 1] for c in range(n)]

        def raw_slot(s):
            if s == EXPERT_RING - 1:
                return cst[:, CONST_AT["decay"]:CONST_AT["decay"] + GCOLS]
            return raw_low[:, s] if s < MIX_RING else raw_high[:, s - MIX_RING]

        def pick(w, k0, n, c0, cols):
            return n, cols, w[k0 * P:(k0 + n) * P, c0:c0 + cols].rearrange("(k p) c -> p k c", p=P)

        def mixer_granule(layer, tile, j):
            w = w_in[layer]
            if tile in ("fq", "fk"):
                return pick(w, 0, 8, START[tile] + 256 * j, 256)
            if tile == "ff":
                return pick(w, 0, 8, START["ff"], HEADS)
            if tile in ("fv", "rq", "rk"):
                return pick(w, 4 * j, 4, START[tile], 512)
            if tile[:2] in ("rv", "rg"):
                return pick(w, 4 * j, 4, START[tile[:2]] + 512 * int(tile[2]), 512)
            if tile == "cq":
                return pick(w, 4 * j, 4, START["cq"], Q_RANK)
            if tile == "ckvkr":
                return pick(w, 4 * j, 4, START["ckv"], KV_RANK + ROPE)
            if tile.startswith("gate"):
                return pick(w, 4 * j, 4, START["gl"] + D * int(tile[4]) + 512 * int(tile[5]), 512)
            if tile[:2] == "uq":
                return pick(mla_w_uq[layer], 0, 3, 384 * int(tile[2]), 384)
            if tile == "uk":
                return pick(mla_w_uk[layer], 0, 2, 0, 512)
            if tile == "uv":
                return pick(mla_w_uv[layer], 0, 2, 0, 512)
            w = dict(fox=w_br_fox, ret=w_br_ret, mla=w_br_mla, out=w_out)[tile[:-1]][layer]
            return pick(w, 4 * j, 4, 512 * int(tile[-1]), 512)

        GRANULE = {}
        for layer in range(DEPTH):
            g = G_MIX[layer]
            for step in PLAN:
                if step[0] == "granule":
                    GRANULE[g] = mixer_granule(layer, step[1], step[2])
                    g += 1

        def dense_granule(p, turn):
            if p < 4:
                w = (dense_w_gate, dense_w_up)[p % 2]
                c0 = turn * 512 + 256 * (p // 2)
                return 8, 256, w[0, :, bass.ds(c0, 256)].rearrange("(k p) c -> p k c", p=P)
            r0 = turn * 512 + 256 * (p - 4)
            return 2, D, dense_w_down[0, bass.ds(r0, 256), :].rearrange("(k p) c -> p k c", p=P)

        def expert_granule(p, e):
            what, i, half = EXPERT_ORDER[p]
            if what == "down":
                rows = slice(FT * i + 256 * half, FT * i + 256 * (half + 1))
                return 2, D, moe_w_down[0, e, rows, :].rearrange("(k p) c -> p k c", p=P)
            w = moe_w_gate if what == "gate" else moe_w_up
            return 4, FT, w[0, e, 512 * half:512 * (half + 1), FT * i:FT * (i + 1)].rearrange(
                "(k p) c -> p k c", p=P)

        def width(g):
            return GRANULE[g][0] * GRANULE[g][1] if g in GRANULE else GCOLS

        def w_parts(g, cols):
            n = width(g) // cols
            return [w[:, g % PAIR_RING, 0:n * cols].rearrange("p (k c) -> p k c", k=n) for w in (w_hi, w_lo)]

        SOURCE_OF = dict(norm0=1, norm1=1, cqT=2, ckvT=2, mqT0=3, mqT1=3, mkT0=4, mkT1=4, rqT=6, rkT=6,
                         oretT0=7, oretT1=7, ffn0=8, ffn1=8)
        SOURCES = 8
        NORMS = 2 * DEPTH
        READS = dict(uq0="cqT", uq1="cqT", uk="ckvT", uv="ckvT")

        def operand(tile):
            if tile in READS:
                hi, lo = (cqT_hi, cqT_lo) if tile[:2] == "uq" else (ckvT_hi, ckvT_lo)
                return hi, lo, (READS[tile],)
            if tile[:-1] == "fox":
                return ofoxT_hi, ofoxT_lo, ()
            if tile[:-1] == "mla":
                return omlaT_hi, omlaT_lo, ()
            if tile[:-1] == "ret":
                return hT_hi, hT_lo, ("oretT0", "oretT1")
            if tile[:-1] == "out":
                return mergedT_hi, mergedT_lo, ("mergedT0", "mergedT1")
            return hT_hi, hT_lo, ("norm0", "norm1")

        def head_rows(buffer, h, cols):
            return buffer[64 * (h % 2):64 * (h % 2) + 64, h // 2, cols]

        def token_dst(tile, b):
            if tile == "ff":
                return forget[:, 0, b, :], HEADS
            if tile[:2] in ("uq", "rv"):
                n, buffer = int(tile[2]), mq[:, b].rearrange("p h d -> p (h d)") if tile[:2] == "uq" else rv[:, b]
                cols = 384 if tile[:2] == "uq" else 512
                return buffer[:, cols * n:cols * (n + 1)], cols
            if tile in ("rq", "rk"):
                return (rq if tile == "rq" else rk)[:, b].rearrange("p h d -> p (h d)"), 512
            buffer = dict(cq=cq, ckvkr=ckvkr, fv=fv, uv=mv)[tile]
            return buffer[:, b], buffer.shape[2]

        def turn_sources(tile):
            if tile[:2] in ("mq", "mk"):
                src = mq if tile[:2] == "mq" else mk
                chunks, rows = [lambda b, h=h: src[:, b, h, :] for h in range(4 * int(tile[3]), 4 * int(tile[3]) + 4)], QK
            else:
                if tile[:-1] in ("norm", "ffn", "oretT"):
                    src, first, n = (o_ret if tile[:-1] == "oretT" else normed), 4 * int(tile[-1]), 4
                elif tile[:-1] == "mergedT":
                    src, first, n = merged[int(tile[-1])], 0, 4
                else:
                    src, first, n = dict(cqT=(cq, 0, 3), ckvT=(ckvkr, 0, 2), rqT=(rq, 0, 4), rkT=(rk, 0, 4))[tile]
                by_token = (lambda b: src[:, b].rearrange("p h d -> p (h d)")) if src in (rq, rk) else (lambda b: src[:, b])
                chunks, rows = [lambda b, c=c: by_token(b)[:, P * c:P * (c + 1)] for c in range(first, first + n)], P
            return [(chunk(b), b, rows) for chunk in chunks for b in range(NB)]

        def turn_target(layer, tile):
            if tile == "cqT":
                return cqT_hi, cqT_lo, channel_weights("qn", layer, 3), 0, 3
            if tile == "ckvT":
                return ckvT_hi, ckvT_lo, channel_weights("kvn", layer, 2), 0, 2
            what = dict(norm="mix", ffn="ffn", oretT="gn", mergedT=None).get(tile[:-1], "plain")
            if what == "plain":
                return None, None, None, 0, 4
            first = 4 * int(tile[-1])
            if what is None:
                return mergedT_hi, mergedT_lo, None, first, 4
            return hT_hi, hT_lo, channel_weights(what, layer, KC)[first:first + 4], first, 4

        def plain_target(tile):
            if tile[:3] in ("mqT", "mkT"):
                first = 4 * int(tile[3])
                return (mqT if tile[:3] == "mqT" else mkT)[:, first:first + 4], QK
            return (rqT if tile == "rqT" else rkT)[:], P

        block = ctx.enter_context(nc.Block())

        @block.sync
        def _(sp):
            sp.dma_start(x_sb[:], x.rearrange("a (b p) d -> p (a b) d", p=P)).then_inc(x_in, 16)
            sp.dma_start(cst[:, 0:FIRST_CONST], consts[:, 0:FIRST_CONST]).then_inc(consts_in, 16)
            at_row = 0
            for w in (norm_mix_w, norm_ffn_w, ret_gn_w, mla_q_norm_w, mla_kv_norm_w):
                rows = w.rearrange("l (c p) -> (l c) p", p=P)
                n = rows.shape[0]
                sp.dma_start(params[at_row:at_row + n, :], rows).then_inc(params_in, 16)
                at_row += n

            def load(g, granule, loaded_before=None):
                s = STREAM.slot[g]
                n, cols, source = granule
                sp.dma_start(raw_slot(s)[:, 0:n * cols].rearrange("p (k c) -> p k c", k=n),
                             source).then_inc(raw_in[s], 16)

            def mixer(layer):
                for g in range(G_MIX[layer], G_MIX[layer] + MIX_G):
                    if STREAM.before[g] is not None:
                        sp.wait_ge(lo_split, STREAM.before[g] + 1)
                    load(g, GRANULE[g])
                    if g == 1:
                        sp.dma_start(forget_bias[:].rearrange("p l h -> p (l h)"),
                                     fox_f_bias.rearrange("l h -> (l h)").partition_broadcast(P)).then_inc(small_in, 16)
                        sp.dma_start(router_raw[:], moe_w_router[0].rearrange("(k p) e -> p k e", p=P)).then_inc(small_in, 16)
                        sp.dma_start(cst[:, FIRST_CONST:], consts[:, FIRST_CONST:]).then_inc(tables_in, 16)

            mixer(0)
            for p in range(DENSE_STEP):
                if p < MIX_RING:
                    sp.wait_ge(lo_split, STREAM.before[G_DENSE + p] + 1)
                else:
                    sp.wait_ge(source_ready, SOURCES)
                load(G_DENSE + p, dense_granule(p, 0))
            with sp.Fori(1, N_DENSE_TURNS) as turn:
                for p in range(DENSE_STEP):
                    sp.wait_ge(lo_split, G_DENSE + p + 1 - DENSE_STEP + turn * DENSE_STEP)
                    load(G_DENSE + p, dense_granule(p, turn))
            mixer(1)
            def expert_load(p, e, E):
                sp.wait_ge(lo_split, E * EXPERT_G + (G_MOE + p + 1 - EXPERT_RING))
                load(G_MOE + p, expert_granule(p % EXPERT_G, e))

            for p in range(EXPERT_G):
                if p < MIX_RING:
                    sp.wait_ge(lo_split, STREAM.before[G_MOE + p] + 1)
                    load(G_MOE + p, expert_granule(p, 0))
                elif p < EXPERT_RING:
                    if p == MIX_RING:
                        sp.wait_ge(source_ready, 2 * SOURCES)
                    load(G_MOE + p, expert_granule(p, 0))
                else:
                    expert_load(p, 0, 0)
            sp.wait_ge(h_lo_ready, 1)
            sp.dma_start(final_row[:], final_norm_w.partition_broadcast(P)).then_inc(final_row_in, 16)
            with sp.Fori(1, N_EXPERTS) as e:
                for p in range(EXPERT_G):
                    expert_load(p, e, e)
            for p in range(AHEAD):
                expert_load(p, 0, N_EXPERTS)
            sp.wait_ge(route_ready, 1)
            many = sp.value_load(most[0:1, 0:1], min_val=0, max_val=SEQ)
            with sp.If(many > P):
                with sp.Fori(0, N_EXPERTS - 1) as e:
                    for p in range(AHEAD, EXPERT_G + AHEAD):
                        expert_load(p, e if p < EXPERT_G else e + 1, e + N_EXPERTS)
                for p in range(AHEAD, EXPERT_G + AHEAD):
                    expert_load(p, N_EXPERTS - 1 if p < EXPERT_G else 0, 2 * N_EXPERTS - 1)
            store = out.rearrange("a (b p) d -> p (a b) d", p=P)
            for b in (1, 0):
                sp.wait_ge(final_done[b], 1)
                sp.dma_start(store[:, b], result[:, b]).then_inc(stored, 16)
            sp.wait_ge(stored, 16 * NB)

        @block.tensor
        def _(pe):
            mm = nc.tensor.matmul

            def three(dst, sides, moving, start, stop):
                mm(dst, sides[0], moving[0], start=start, stop=False)
                mm(dst, sides[0], moving[1], start=False, stop=False)
                return mm(dst, sides[1], moving[0], start=False, stop=stop)

            def split_arrived(g):
                pe.wait_ge(hi_split, g + 1)
                pe.wait_ge(lo_split, g + 1)

            def tile_done(layer, tile):
                pe.wait_ge(tile_act, TILES.act[layer, tile])
                pe.wait_ge(tile_dve, TILES.dve[layer, tile])

            def banks_free(layer, tile):
                if TILES.before[layer, tile]:
                    tile_done(*TILES.before[layer, tile])

            def granule(layer, g, tile, j, last):
                bank = TILES.bank[layer, tile]
                hi, lo, ready = operand(tile)
                n, cols, _ = GRANULE[g]
                if j < len(ready):
                    tile_done(layer, ready[0 if n == KC else j])
                if j == 0:
                    banks_free(layer, tile)
                    if tile[:-1] == "fox":
                        pe.wait_ge(heads_act, 4 * layer + 2)
                        pe.wait_ge(heads_dve, 4 * layer + 2)
                    if tile[:-1] == "mla":
                        pe.wait_ge(heads_act, 4 * layer + 4)
                        pe.wait_ge(heads_dve, 4 * layer + 4)
                split_arrived(g)
                wh, wl = w_parts(g, cols)
                if tile in ("fq", "fk"):
                    for c in range(2):
                        for k in range(n):
                            if c == 0 and k == 4:
                                tile_done(layer, ready[1])
                            i = three(ps[:, bank + j, SEQ * c:SEQ * (c + 1)],
                                      [w[:, k, P * c:P * (c + 1)] for w in (wh, wl)],
                                      (hi[:, k, :], lo[:, k, :]), k == 0, k == n - 1)
                else:
                    for b in range(NB):
                        for k in range(n):
                            kk = 4 * j + k
                            if n == KC and b == 0 and k == 4:
                                tile_done(layer, ready[1])
                            i = three(ps[:, bank + b, 0:cols], [s[:, kk, P * b:P * (b + 1)] for s in (hi, lo)],
                                      (wh[:, k, :], wl[:, k, :]), kk == 0, last and k == n - 1)
                i.then_inc(granule_used, 1)

            def turn(layer, tile):
                banks_free(layer, tile)
                if tile[:-1] == "mergedT":
                    tile_done(layer, "ret" + tile[-1])
                else:
                    pe.wait_ge(source_ready, SOURCES * layer + SOURCE_OF[tile])
                    if tile[:-1] in ("norm", "ffn"):
                        pe.wait_ge(normed_act, 2 * layer + 1 + (tile[:-1] == "ffn"))
                bank = TILES.bank[layer, tile]
                for c, (src, b, rows) in enumerate(turn_sources(tile)):
                    i = nc.tensor.transpose(ps[0:rows, bank + c // 4, P * (c % 4):P * (c % 4 + 1)], src, ident)
                i.then_inc(turned_ready, 1)

            def scores(layer, k):
                h = k % HEADS
                fox = k < HEADS
                if use_of_6(layer, "softmax", k):
                    pe.wait_ge(scores_taken, use_of_6(layer, "softmax", k))
                if k == 0:
                    tile_done(layer, "fq")
                    tile_done(layer, "fk")
                    pe.wait_ge(neg_cum_ready, layer + 1)
                if k == HEADS:
                    tile_done(layer, "mkT1")
                for b in range(NB):
                    keys = P * (b + 1)
                    dst = ps[:, 6, P * b:P * b + keys]
                    queries = slice(P * b, P * (b + 1))
                    if fox:
                        mm(dst, head_rows(fqT, h, queries), head_rows(fkT, h, slice(0, keys)),
                           start=True, stop=False)
                        pick_h = pick_head[:, h:h + 1]
                        for part in (cum_hi, cum_lo):
                            mm(dst, part[:, queries], pick_h.broadcast_to([P, keys]), start=False, stop=False)
                        for part in (neg_hi, neg_lo):
                            i = mm(dst, pick_h.broadcast_to([P, P]), part[:, 0:keys], start=False, stop=part is neg_lo)
                    else:
                        i = mm(dst, mqT[0:QK, h, queries], mkT[0:QK, h, 0:keys], start=True, stop=True)
                i.then_inc(scores_ready, 1)

            def turn_probs(layer, k):
                pe.wait_ge(prob_ready, 16 * layer + k + 1)
                free = use_of_7(layer, "softmax", k)
                if free:
                    pe.wait_ge(right_act, free)
                for c in range(3):
                    i = nc.tensor.transpose(ps[:, 7, P * c:P * (c + 1)], prob[:, k % 2, P * c:P * (c + 1)], ident)
                i.then_inc(right_ready, 1)

            def values(layer, k):
                h = k % HEADS
                unit = 4 * layer + k // 4
                if k % 4 == 0 and unit >= 2:
                    pe.wait_ge(heads_act, unit - 1)
                    pe.wait_ge(heads_dve, unit - 1)
                pe.wait_ge(right_act, use_of_7(layer, "softmax", k) + 1)
                if k == 0:
                    tile_done(layer, "fv")
                if k == HEADS:
                    tile_done(layer, "uv")
                v = fv if k < HEADS else mv
                dst = ps[64 * (h % 2):64 * (h % 2) + 64, 4 + unit % 2,
                         SEQ * (h // 2 % 2):SEQ * (h // 2 % 2 + 1)]
                vh = slice(64 * h, 64 * h + 64)
                pt = prob_T[:, k % 2]
                mm(dst[:, 0:P], v[:, 0, vh], pt[:, 0:P], start=True, stop=True)
                mm(dst[:, P:2 * P], v[:, 0, vh], pt[:, P:2 * P], start=True, stop=False)
                i = mm(dst[:, P:2 * P], v[:, 1, vh], pt[:, 2 * P:3 * P], start=False, stop=True)
                if k % 4 == 3:
                    i.then_inc(heads_ready, 1)

            def retention_scores(layer, r):
                pe.wait_ge(scores_taken, use_of_6(layer, "retention", r))
                if r == 0:
                    tile_done(layer, "rqT")
                    tile_done(layer, "rkT")
                mm(ps[:, 6, 0:SEQ], head_rows(rkT, r, slice(0, P)), head_rows(rqT, r, slice(0, SEQ)),
                   start=True, stop=True)
                mm(ps[:, 6, SEQ:SEQ + P], head_rows(rkT, r, slice(P, SEQ)), head_rows(rqT, r, slice(P, SEQ)),
                   start=True, stop=True).then_inc(scores_ready, 1)

            def retention_values(layer, r):
                pe.wait_ge(scores_taken, use_of_6(layer, "retention", r) + 1)
                pe.wait_ge(right_act, use_of_7(layer, "retention", r))
                if r == 0:
                    tile_done(layer, "rv1")
                pt = prob_T[:, r % 2]
                vh = slice(RET_V * r, RET_V * (r + 1))
                mm(ps[:, 7, 0:P], pt[:, 0:P], rv[:, 0, vh], start=True, stop=True)
                mm(ps[:, 7, P:2 * P], pt[:, P:2 * P], rv[:, 0, vh], start=True, stop=False)
                mm(ps[:, 7, P:2 * P], pt[:, 2 * P:3 * P], rv[:, 1, vh], start=False, stop=True).then_inc(right_ready, 1)

            def side(layer, what, k):
                if what == "cumulate":
                    pe.wait_ge(forget_ready, layer + 1)
                    free = use_of_7(layer, "cumulate", 0)
                    if free:
                        pe.wait_ge(right_act, free)
                    mm(ps[:, 7, 0:P], log_f[:, 0], cum[:, 0:P], start=True, stop=True)
                    mm(ps[:, 7, P:2 * P], log_f[:, 0], cum[:, P:2 * P], start=True, stop=False)
                    mm(ps[:, 7, P:2 * P], log_f[:, 1], cum[:, 0:P], start=False, stop=True).then_inc(right_ready, 1)
                elif what == "softmax":
                    if k < 16:
                        scores(layer, k)
                    if 1 <= k < 17:
                        turn_probs(layer, k - 1)
                    if k >= 2:
                        values(layer, k - 2)
                elif what == "retention":
                    if k < HEADS:
                        retention_scores(layer, k)
                    if k:
                        retention_values(layer, k - 1)

            def mixer(layer):
                g = G_MIX[layer]
                for step in PLAN:
                    if step[0] == "granule":
                        granule(layer, g, *step[1:])
                        g += 1
                    elif step[0] == "turn":
                        turn(layer, step[1])
                    else:
                        side(layer, *step[1:])

            pe.wait_ge(consts_in, 16)
            pe.wait_ge(params_in, 16 * 5)
            nc.tensor.transpose(ps[:, 4, 0:N_PARAM], params[:], ident[0:N_PARAM, 0:N_PARAM]).then_inc(params_turned, 1)
            pe.wait_ge(zeroed, 1)
            mixer(0)

            tile_done(0, "ffn1")
            for bank in range(4, 8):
                mm(ps[:, bank, :], zeros[:], hT_hi[:, 0:2, :].rearrange("p k t -> p (k t)"), start=True, stop=False)
            with pe.Fori(0, N_DENSE_TURNS) as turn_no:
                g0 = turn_no * DENSE_STEP
                for p in range(DENSE_STEP):
                    g = G_DENSE + p
                    pe.wait_ge(hi_split, g0 + g + 1)
                    pe.wait_ge(lo_split, g0 + g + 1)
                    i2 = p // 2 if p < 4 else p - 4
                    if p < 4:
                        if p % 2 == 0:
                            pe.wait_ge(d_act_ready, turn_no * 2 + i2 + 1)
                        wh, wl = w_parts(g, 256)
                        for c in range(2):
                            for k in range(KC):
                                i = three(ps[:, p, SEQ * c:SEQ * (c + 1)],
                                          [w[:, k, P * c:P * (c + 1)] for w in (wh, wl)],
                                          (hT_hi[:, k, :], hT_lo[:, k, :]), k == 0, k == KC - 1)
                    else:
                        pe.wait_ge(d_hi_ready, turn_no * 2 + i2 + 1)
                        pe.wait_ge(d_lo_ready, turn_no * 2 + i2 + 1)
                        wh, wl = w_parts(g, D)
                        for c in range(2):
                            for b in range(NB):
                                for n in range(2):
                                    tok = slice(SEQ * c + P * b, SEQ * c + P * (b + 1))
                                    i = three(ps[:, 4 + 2 * b + n, :],
                                              (d_act_hi[:, i2, tok], d_act_lo[:, i2, tok]),
                                              (wh[:, c, 512 * n:512 * (n + 1)], wl[:, c, 512 * n:512 * (n + 1)]),
                                              False, False)
                    i.then_inc(granule_used, 1)
            for bank in range(4, 8):
                i = mm(ps[:, bank, :], zeros[:], hT_hi[:, 0:2, :].rearrange("p k t -> p (k t)"), start=False, stop=True)
            i.then_inc(d_summed, 1)
            mixer(1)

            pe.wait_ge(router_hi_ready, 1)
            pe.wait_ge(router_lo_ready, 1)
            for k in range(KC):
                if k % 4 == 0:
                    tile_done(1, f"ffn{k // 4}")
                for part in (hT_hi, hT_lo):
                    i = mm(ps[0:2 * N_EXPERTS, 6, 0:SEQ], router_w[:, k].rearrange("p a e -> p (a e)"), part[:, k],
                           start=k == 0 and part is hT_hi, stop=k == KC - 1 and part is hT_lo)
            i.then_inc(logits_ready, 1)
            pe.wait_ge(logits_copied, 1)
            for b in range(NB):
                i = nc.tensor.transpose(ps[:, 7, 2 * N_EXPERTS * b:2 * N_EXPERTS * (b + 1)],
                                        logits_T[:, P * b:P * (b + 1)], ident[0:2 * N_EXPERTS, 0:2 * N_EXPERTS])
            i.then_inc(logits_turned, 1)
            for bank in (4, 5):
                mm(ps[:, bank, :], zeros[:], hT_hi[:, 0:2, :].rearrange("p k t -> p (k t)"), start=True, stop=True)
            pe.wait_ge(chosen_ready, 1)
            own, whole = cum_01[:, 0:P], cum_01[:, P:2 * P]
            E8 = N_EXPERTS
            mm(ps[:, 6, 0:E8], own, chosen_01[:, 0], start=True, stop=True)
            mm(ps[:, 6, E8:2 * E8], whole, chosen_01[:, 0], start=True, stop=False)
            mm(ps[:, 6, E8:2 * E8], own, chosen_01[:, 1], start=False, stop=True).then_inc(ranks_ready, 1)
            mm(ps[:, 7, 0:E8], whole, chosen_01[:, 0], start=True, stop=False)
            mm(ps[:, 7, 0:E8], whole, chosen_01[:, 1], start=False, stop=True).then_inc(counts_ready, 1)

            def misc_bank(u, E, half):
                by_act, by_dve = misc_taken(u - 2, E, half)
                pe.wait_ge(misc_act, by_act)
                pe.wait_ge(misc_dve, by_dve)
                return 6 + u % 2

            def gather(E, part):
                pe.wait_ge(onehot_ready, E + 1)
                for k in range(4 * part, 4 * part + 4):
                    for b in range(NB):
                        for h in (h_hi, h_lo):
                            i = mm(ps[:, 2 + part, P * (k % 4):P * (k % 4 + 1)],
                                   h[:, b, P * k:P * (k + 1)], onehot[:, b],
                                   start=b == 0 and h is h_hi, stop=b == NB - 1 and h is h_lo)
                i.then_inc(gathered, 1)

            def scatter(E, half):
                pe.wait_ge(y_hi_ready, E + (1 + half))
                pe.wait_ge(y_lo_ready, E + (1 + half))
                for u in range(N_PARTS):
                    b, n = u // 2, u % 2
                    bank = misc_bank(u, E, half)
                    cols = slice(512 * n, 512 * (n + 1))
                    tok = slice(P * b, P * (b + 1))
                    mm(ps[:, bank, :], onehot_T[:, tok], y_hi[:, cols], start=True, stop=False)
                    mm(ps[:, bank, :], onehot_T[:, tok], y_lo[:, cols], start=False, stop=True).then_inc(misc_ready, 1)

            def expert(E, half):
                def turn_act(i):
                    pe.wait_ge(e_act_ready, E * N_FT + (i + 1))
                    bank = misc_bank(N_PARTS + 1 + i, E, half)
                    for c in range(4):
                        t = nc.tensor.transpose(ps[:, bank, P * c:P * (c + 1)], e_act[:, i % 2, P * c:P * (c + 1)], ident)
                    t.then_inc(misc_ready, 1)

                pe.wait_ge(xg_lo_ready, E * 2 + 2)
                for p, (what, i, part) in enumerate(EXPERT_ORDER):
                    g = G_MOE + p
                    if what == "gate" and part == 0 and i >= 2:
                        pe.wait_ge(e_act_ready, E * N_FT + (i - 1))
                    if what == "down" and part == 0:
                        if i == N_FT - 1:
                            turn_act(i)
                            gather(E + 1, 1)
                        by_act, by_dve = misc_taken(N_PARTS + 1 + i, E, half)
                        pe.wait_ge(misc_act, by_act)
                        pe.wait_ge(misc_dve, by_dve)
                    pe.wait_ge(hi_split, E * EXPERT_G + (g + 1))
                    pe.wait_ge(lo_split, E * EXPERT_G + (g + 1))
                    if what == "down":
                        wh, wl = w_parts(g, D)
                        for c in range(2):
                            f = 2 * part + c
                            for n in range(2):
                                cols = slice(512 * n, 512 * (n + 1))
                                m = three(ps[:, 4 + n, :], (e_actT_hi[:, i % 2, f], e_actT_lo[:, i % 2, f]),
                                          (wh[:, c, cols], wl[:, c, cols]), i == 0 and f == 0,
                                          i == N_FT - 1 and f == 3)
                    else:
                        bank = 2 * (i % 2) + (what == "up")
                        wh, wl = w_parts(g, FT)
                        for k in range(4):
                            kk = 4 * part + k
                            m = three(ps[:, bank, :], (xg_hi[:, kk], xg_lo[:, kk]), (wh[:, k], wl[:, k]),
                                      kk == 0, kk == KC - 1)
                    m.then_inc(granule_used, 1)
                    if what == "gate" and part == 1:
                        if i == 0:
                            scatter(E, half)
                        else:
                            turn_act(i - 1)
                    if what == "up" and part == 1 and i == 0:
                        bank = misc_bank(N_PARTS, E, half)
                        for b in range(NB):
                            t = nc.tensor.transpose(ps[:, bank, P * b:P * (b + 1)], onehot.bitcast(F32)[:, b], ident)
                        t.then_inc(misc_ready, 1)
                    if what == "up" and part == 1 and i == N_FT - 1:
                        pe.wait_ge(e_act_ready, E * N_FT + (N_FT - 1))
                        gather(E + 1, 0)

            def expert_pass(half):
                with pe.Fori(0, N_EXPERTS) as e:
                    expert(e + N_EXPERTS * half if half else e, half)
                scatter(N_EXPERTS * (half + 1), half)

            pe.wait_ge(h_lo_ready, 1)
            gather(0, 0)
            gather(0, 1)
            expert_pass(0)
            many = pe.value_load(most[0:1, 0:1], min_val=0, max_val=SEQ)
            with pe.If(many > P):
                expert_pass(1)

        @block.scalar
        def _(act):
            af = nc.scalar.activation
            steps = [0]

            def then(i):
                steps[0] += 1
                i.then_inc(act_step, 1)
                act.wait_ge(act_step, steps[0])

            def split(g, turn=0, loads=0, used=0):
                s = STREAM.slot[g]
                act.wait_ge(raw_in[s], turn * (16 * loads) + 16 * STREAM.loads[g])
                if g >= PAIR_RING:
                    act.wait_ge(granule_used, turn * used + (g - PAIR_RING + 1))
                n = width(g)
                af(w_hi[:, g % PAIR_RING, 0:n], raw_slot(s)[:, 0:n], ACT.Copy).then_inc(hi_split, 1)

            def table_of(function):
                af(table_loaded[:], eps_col[:], function)

            norms = [0]

            def deviations(pieces, dims):
                for i, (piece, scratch) in enumerate(pieces):
                    last = af(scratch, piece, ACT.Square, accum_out=stat[:, i:i + 1])
                then(last)
                for i, (n, dim) in enumerate(dims):
                    a = sum(m for m, _ in dims[:i])
                    last = af(stat[:, 16 + a:16 + a + n], stat[:, a:a + n], ACT.Sqrt, bias=eps_col[:],
                              scale=1.0 / dim)
                last.then_inc(deviation, 1)

            def tile_dve_done(layer, tile):
                act.wait_ge(tile_dve, TILES.dve[layer, tile])

            def take(layer, tile, g):
                bank = TILES.bank[layer, tile]
                if not takers(tile)[0]:
                    return
                act.wait_ge(granule_used, g + 1)
                if tile == "fq":
                    i = af(fqT[:, 0:2], ps[:, bank].rearrange("p (c t) -> p c t", c=2), ACT.Copy, scale=FOX_D ** -0.5)
                elif tile == "fk":
                    i = af(fkT[:, 0:2], ps[:, bank].rearrange("p (c t) -> p c t", c=2), ACT.Copy)
                elif tile == "uk":
                    i = af(mk[:, 0, :, 0:NOPE], ps[:, bank].rearrange("p (h d) -> p h d", h=HEADS), ACT.Copy)
                elif tile in ("rg0", "rg1"):
                    n = int(tile[2])
                    i = af(rg[:, :, 512 * n:512 * (n + 1)], ps[:, bank:bank + 2, :], ACT.Silu)
                elif tile.startswith("gate"):
                    i = af(gates[gate_slot(tile)][:], ps[:, bank:bank + 2, :], ACT.Sigmoid)
                else:
                    dst, cols = token_dst(tile, 0)
                    i = af(dst, ps[:, bank, 0:cols], ACT.Copy)
                i.then_inc(tile_act, 1)

            def turned_tile(layer, tile):
                act.wait_ge(turned_ready, turn_count(layer, tile))
                bank = TILES.bank[layer, tile]
                hi, _, weights, first, n = turn_target(layer, tile)
                if weights is None and hi is None:
                    dst, rows = plain_target(tile)
                    i = af(dst[0:rows, 0:2], ps[0:rows, bank].rearrange("p (c t) -> p c t", c=2), ACT.Copy)
                else:
                    for c in range(n):
                        src = ps[:, bank + c // 2, SEQ * (c % 2):SEQ * (c % 2 + 1)]
                        if weights is None:
                            i = af(hi[:, first + c], src, ACT.Copy)
                        else:
                            i = af(hi[:, first + c], src, ACT.Copy, scale=weights[c])
                        if c == 1 and n == 4:
                            i.then_inc(first_bank_hi, 1)
                i.then_inc(tile_act, 1)

            def heads_split(layer, u):
                act.wait_ge(heads_ready, 4 * layer + u + 1)
                hi = ofoxT_hi if u < 2 else omlaT_hi
                af(hi[:, 2 * (u % 2):2 * (u % 2) + 2], ps[:, 4 + u % 2].rearrange("p (c t) -> p c t", c=2),
                   ACT.Copy).then_inc(heads_act, 1)

            def side(layer, what, k):
                if what in ("norm_mix", "norm_ffn"):
                    table_of(ACT.Sqrt)
                    if what == "norm_mix" and layer == 0:
                        act.wait_ge(x_in, 16)
                    elif what == "norm_mix":
                        act.wait_ge(x_summed, 1)
                    else:
                        tile_dve_done(layer, "out1")
                    norms[0] += 1
                    then(af(normed[:, 0], x_sb[:, 0], ACT.Square, accum_out=stat[:, 0:1]))
                    act.wait_ge(squares_dve, norms[0])
                    af(stat[:, 16:16 + NB], stat[:, 0:NB], ACT.Sqrt, bias=eps_col[:], scale=1.0 / D).then_inc(deviation, 1)
                    act.wait_ge(inverse_ready, norms[0])
                    af(normed[:, 0], x_sb[:, 0], ACT.Copy, scale=stat[:, 24:25]).then_inc(normed_act, 1)
                    if what == "norm_ffn" and layer == 1:
                        act.wait_ge(normed_act, NORMS)
                        act.wait_ge(source_ready, 2 * SOURCES)
                        af(h_hi[:], normed[:], ACT.Copy).then_inc(h_hi_ready, 1)
                elif what == "forget":
                    act.wait_ge(logits_abs, layer + 1)
                    then(af(forget[:, 2], forget[:, 1], ACT.Exp, scale=-1.0))
                    af(forget[:, 3], forget[:, 2], ACT.Ln, bias=1.0).then_inc(log_terms, 1)
                elif what == "latent_norm":
                    tile_dve_done(layer, "cq")
                    tile_dve_done(layer, "ckvkr")
                    act.wait_ge(tile_act, TILES.act[layer, "ckvkr"])
                    deviations([(cq[:, b], latent_scratch[:, b]) for b in range(NB)]
                               + [(ckvkr[:, b, 0:KV_RANK], latent_scratch[:, NB + b, 0:KV_RANK]) for b in range(NB)],
                               [(NB, Q_RANK), (NB, KV_RANK)])
                elif what == "cumulate":
                    if layer == 0:
                        act.wait_ge(small_in, 16 * 2)
                        af(router_w[:, :, 0], router_raw[:], ACT.Copy).then_inc(router_hi_ready, 1)
                    act.wait_ge(right_ready, use_of_7(layer, "cumulate", 0) + 1)
                    if layer == 0:
                        af(pick_head[:], ident[:, 0:HEADS], ACT.Copy)
                        af(cum_01[:], cum, ACT.Copy)
                    af(neg_hi[:], ps[:, 7, 0:SEQ], ACT.Copy, scale=-1.0)
                    af(cum_hi[:], ps[:, 7, 0:SEQ], ACT.Copy).then_inc(right_act, 1)
                elif what == "softmax":
                    if k < 16:
                        n = 16 * layer + k
                        act.wait_ge(row_max_ready, n + 1)
                        for b in range(NB):
                            cols = slice(P * b, P * b + P * (b + 1))
                            i = af(prob[:, k % 2, cols], prob[:, k % 2, cols], ACT.Exp,
                                   bias=stat[:, 34 + 2 * (k % 2) + b:35 + 2 * (k % 2) + b],
                                   accum_out=stat[:, 38 + 2 * (k % 2) + b:39 + 2 * (k % 2) + b])
                        i.then_inc(prob_exp, 1)
                    if 1 <= k < 17:
                        act.wait_ge(right_ready, use_of_7(layer, "softmax", k - 1) + 1)
                        af(prob_T[:, (k - 1) % 2], ps[:, 7, 0:384], ACT.Copy).then_inc(right_act, 1)
                    if k >= 2 and (k - 2) % 4 == 3:
                        heads_split(layer, (k - 2) // 4)
                elif what == "retention" and k:
                    act.wait_ge(right_ready, use_of_7(layer, "retention", k - 1) + 1)
                    af(o_ret[:, :, RET_V * (k - 1):RET_V * k], ps[:, 7, 0:SEQ].rearrange("p (b e) -> p b e", b=NB),
                       ACT.Copy).then_inc(right_act, 1)
                elif what == "ret_norm":
                    act.wait_ge(ret_var_ready, HEADS * (layer + 1))
                    af(ret_dev[:], ret_stat[:, :, :, 1], ACT.Sqrt, bias=eps_col[:]).then_inc(ret_dev_ready, 1)

            def start():
                act.wait_ge(params_turned, 1)
                af(param_T[:], ps[:, 4, 0:N_PARAM], ACT.Copy).then_inc(params_ready, 1)
                act.wait_ge(params_ready, 1)
                split(0)

            def mixer(layer):
                g = G_MIX[layer]
                for step in PLAN:
                    if layer == 0 and step == ("turn", "norm0"):
                        start()
                    if step[0] == "granule":
                        split(g + AHEAD)
                        if step[3]:
                            take(layer, step[1], g)
                        g += 1
                    elif step[0] == "turn":
                        turned_tile(layer, step[1])
                        if layer == 0 and step[1] == "norm1":
                            split(1)
                    else:
                        side(layer, *step[1:])

            act.wait_ge(zeroed, 1)
            mixer(0)

            with act.Fori(0, N_DENSE_TURNS) as turn_no:
                table_of(ACT.Silu)
                def silu(i):
                    act.wait_ge(granule_used, turn_no * DENSE_STEP + (G_DENSE + 2 * i + 1))
                    af(d_silu[:, i], ps[:, 2 * i, :], ACT.Silu).then_inc(d_silu_ready, 1)

                def hi_part(i):
                    act.wait_ge(d_act_ready, turn_no * 2 + (i + 3))
                    af(d_act_hi[:, i], d_act[:, i], ACT.Copy).then_inc(d_hi_ready, 1)

                for p in range(DENSE_STEP):
                    split(G_DENSE + p + AHEAD, turn_no, 1, DENSE_STEP)
                    if p == 0:
                        silu(0)
                    if p == 2:
                        hi_part(0)
                        silu(1)
                    if p == 4:
                        hi_part(1)
            mixer(1)

            act.wait_ge(logits_ready, 1)
            af(logits_T[:], ps[0:2 * N_EXPERTS, 6, 0:SEQ], ACT.Copy).then_inc(logits_copied, 1)
            act.wait_ge(logit_max_ready, 1)
            for b in range(NB):
                i = af(rt[:, EXPS, b], rt[:, LOGITS, b], ACT.Exp, bias=stat[:, 44 + b:45 + b])
            i.then_inc(logit_exp, 1)
            ffn_weights = channel_weights("ffn", 1, KC)

            def gathered_part(E, part):
                act.wait_ge(gathered, E * 2 + (part + 1))
                for k in range(4 * part, 4 * part + 4):
                    i = af(xg_hi[:, k], ps[:, 2 + part, P * (k % 4):P * (k % 4 + 1)], ACT.Copy, scale=ffn_weights[k])
                i.then_inc(xg_hi_ready, 1)

            def result_part(E, half):
                if half:
                    act.wait_ge(misc_dve, misc_taken(-1, E, half)[1])
                act.wait_ge(granule_used, E * EXPERT_G + G_MOE)
                af(y_hi[:].rearrange("p (a c) -> p a c", a=2), ps[:, 4:6, :], ACT.Copy).then_inc(y_hi_ready, 1)

            def expert(E, half):
                uses = E * MISC_USES + (N_PARTS * half + 1)

                def turned_hi(i):
                    u = N_PARTS + 1 + i
                    act.wait_ge(misc_ready, uses + u)
                    af(e_actT_hi[:, i % 2].rearrange("p a b -> p (a b)"), ps[:, 6 + u % 2, :],
                       ACT.Copy).then_inc(misc_act, 1)

                for p, (what, i, part) in enumerate(EXPERT_ORDER):
                    split(G_MOE + p + AHEAD, E, EXPERT_G // EXPERT_RING, EXPERT_G)
                    if p == 0:
                        result_part(E, half)
                    if what == "gate" and part == 1:
                        act.wait_ge(granule_used, E * EXPERT_G + (G_MOE + p + 1))
                        af(e_silu[:, i % 2], ps[:, 2 * (i % 2), :], ACT.Silu).then_inc(e_silu_ready, 1)
                        if i >= 1:
                            turned_hi(i - 1)
                    if what == "up" and part == 1 and i == 0:
                        act.wait_ge(misc_ready, uses + N_PARTS)
                        af(onehot_T[:], ps[:, 6 + N_PARTS % 2, 0:SEQ], ACT.Copy).then_inc(misc_act, 1)
                    if what == "up" and part == 1 and i == N_FT - 1:
                        gathered_part(E + 1, 0)
                    if what == "down" and part == 1 and i == N_FT - 2:
                        turned_hi(N_FT - 1)
                        gathered_part(E + 1, 1)

            act.sem_inc(misc_act, 1)
            gathered_part(0, 0)
            gathered_part(0, 1)
            with act.Fori(0, N_EXPERTS) as e:
                table_of(ACT.Silu)
                expert(e, 0)
            result_part(N_EXPERTS, 0)
            act.wait_ge(route_ready, 1)
            many = act.value_load(most[0:1, 0:1], min_val=0, max_val=SEQ)
            with act.If(many > P):
                with act.Fori(0, N_EXPERTS) as e:
                    table_of(ACT.Silu)
                    expert(e + N_EXPERTS, 1)
                result_part(2 * N_EXPERTS, 1)
            table_of(ACT.Sqrt)
            act.wait_ge(final_in, 1)
            for b in range(NB):
                last = af(final_scratch[:, b], x_sb[:, b], ACT.Square, accum_out=stat[:, b:b + 1])
            last.then_inc(final_sq, 1)
            act.wait_ge(final_sq, 1)
            af(stat[:, 16:16 + NB], stat[:, 0:NB], ACT.Sqrt, bias=eps_col[:], scale=1.0 / D).then_inc(deviation, 1)
            act.wait_ge(inverse_ready, NORMS + 1)
            af(result[:, 0], result[:, 0], ACT.Copy, scale=stat[:, 24:25]).then_inc(final_done[0], 1)

        @block.vector
        def _(dve):
            v = nc.vector
            steps = [0]

            def then(i):
                steps[0] += 1
                i.then_inc(dve_step, 1)
                dve.wait_ge(dve_step, steps[0])

            def split(g, turn=0, loads=0, used=0):
                s = STREAM.slot[g]
                dve.wait_ge(hi_split, turn * used + (g + 1))
                n = width(g)
                v.tensor_tensor(w_lo[:, g % PAIR_RING, 0:n], raw_slot(s)[:, 0:n],
                                w_hi.bitcast(F32)[:, g % PAIR_RING, 0:n], ALU.subtract).then_inc(lo_split, 1)

            norms, halves = [0], [0]

            def scales(n):
                norms[0] += 1
                dve.wait_ge(deviation, norms[0])
                then(v.reciprocal(stat[:, 24:24 + n], stat[:, 16:16 + n]))

            def tile_act_done(layer, tile):
                dve.wait_ge(tile_act, TILES.act[layer, tile])

            def take(layer, tile, g):
                bank = TILES.bank[layer, tile]
                if not takers(tile)[1]:
                    return
                dve.wait_ge(granule_used, g + 1)
                if tile == "fq":
                    i = v.tensor_scalar(fqT[:, 2:4], ps[:, bank + 1].rearrange("p (c t) -> p c t", c=2),
                                        FOX_D ** -0.5, None, ALU.mult)
                elif tile == "fk":
                    i = v.tensor_copy(fkT[:, 2:4], ps[:, bank + 1].rearrange("p (c t) -> p c t", c=2))
                elif tile == "uk":
                    i = v.tensor_copy(mk[:, 1, :, 0:NOPE], ps[:, bank + 1].rearrange("p (h d) -> p h d", h=HEADS))
                elif tile[:-1] in ("fox", "ret", "mla"):
                    branch, half = ("fox", "ret", "mla").index(tile[:-1]), int(tile[-1])
                    gate = f"gate{branch}{half}"
                    tile_act_done(layer, gate)
                    src = ps[:, bank:bank + 2, :]
                    if branch == 0:
                        i = v.tensor_tensor(merged[half][:], gates[gate_slot(gate)][:], src, ALU.mult)
                    else:
                        dve.wait_ge(tile_dve, TILES.dve[layer, tile] - 1)
                        then(v.tensor_tensor(mixed[:], gates[gate_slot(gate)][:], src, ALU.mult))
                        i = v.tensor_tensor(merged[half][:], merged[half][:], mixed[:], ALU.add)
                elif tile[:-1] == "out":
                    cols = slice(512 * int(tile[-1]), 512 * (int(tile[-1]) + 1))
                    i = v.tensor_tensor(x_sb[:, :, cols], x_sb[:, :, cols], ps[:, bank:bank + 2, :], ALU.add)
                else:
                    dst, cols = token_dst(tile, 1)
                    i = v.tensor_copy(dst, ps[:, bank + 1, 0:cols])
                i.then_inc(tile_dve, 1)

            def turned_tile(layer, tile):
                bank = TILES.bank[layer, tile]
                hi, lo, weights, first, n = turn_target(layer, tile)
                if hi is None:
                    dve.wait_ge(turned_ready, turn_count(layer, tile))
                    dst, rows = plain_target(tile)
                    i = v.tensor_copy(dst[0:rows, 2:4], ps[0:rows, bank + 1].rearrange("p (c t) -> p c t", c=2))
                else:
                    for c in range(n):
                        if n == 4 and c == 0:
                            dve.wait_ge(first_bank_hi, WIDE_SPLITS[layer, tile] + 1)
                        elif c == 2 or n < 4 and c == 0:
                            tile_act_done(layer, tile)
                        src = ps[:, bank + c // 2, SEQ * (c % 2):SEQ * (c % 2 + 1)]
                        was = hi.bitcast(F32)[:, first + c]
                        if weights is None:
                            i = v.tensor_tensor(lo[:, first + c], src, was, ALU.subtract)
                        else:
                            i = v.scalar_tensor_tensor(lo[:, first + c], src, weights[c], was, ALU.mult, ALU.subtract)
                i.then_inc(tile_dve, 1)

            def rope(t, half, cos, sin):
                c = cos.rearrange("p (b d) -> p b d", b=NB).unsqueeze(2)
                s = sin.rearrange("p (b d) -> p b d", b=NB).unsqueeze(2)
                n = t.shape[2]
                tmp = turned[:, :, 0:n, 0:2 * half]
                v.tensor_tensor(tmp[:, :, :, 0:half], t[:, :, :, half:], s[:, :, :, 0:half].broadcast_to([P, NB, n, half]), ALU.mult)
                then(v.tensor_tensor(tmp[:, :, :, half:], t[:, :, :, 0:half], s[:, :, :, half:].broadcast_to([P, NB, n, half]), ALU.mult))
                then(v.tensor_tensor(t, t, c.broadcast_to([P, NB, n, 2 * half]), ALU.mult))
                return v.tensor_tensor(t, t, tmp, ALU.add)

            def heads_split(layer, u):
                dve.wait_ge(heads_act, 4 * layer + u + 1)
                hi, lo = (ofoxT_hi, ofoxT_lo) if u < 2 else (omlaT_hi, omlaT_lo)
                cs = slice(2 * (u % 2), 2 * (u % 2) + 2)
                v.tensor_tensor(lo[:, cs], ps[:, 4 + u % 2].rearrange("p (c t) -> p c t", c=2),
                                hi.bitcast(F32)[:, cs], ALU.subtract).then_inc(heads_dve, 1)

            def side(layer, what, k):
                if what in ("norm_mix", "norm_ffn"):
                    if what == "norm_mix" and layer == 0:
                        dve.wait_ge(x_in, 16)
                    elif what == "norm_ffn":
                        dve.wait_ge(tile_dve, TILES.dve[layer, "out1"])
                    v.tensor_tensor_reduce(out=normed[:, 1], in0=x_sb[:, 1], in1=x_sb[:, 1], scale=1.0, scalar=0.0,
                                           op0=ALU.mult, op1=ALU.add, accum_out=stat[:, 1:2]).then_inc(squares_dve, 1)
                    norms[0] += 1
                    dve.wait_ge(deviation, norms[0])
                    v.reciprocal(stat[:, 24:24 + NB], stat[:, 16:16 + NB]).then_inc(inverse_ready, 1)
                    halves[0] += 1
                    dve.wait_ge(inverse_ready, halves[0])
                    v.tensor_scalar(normed[:, 1], x_sb[:, 1], stat[:, 25:26], None, ALU.mult).then_inc(source_ready, 1)
                elif what == "forget":
                    tile_act_done(layer, "ff")
                    dve.wait_ge(tile_dve, TILES.dve[layer, "ff"])
                    dve.wait_ge(small_in, 16 * 2)
                    dve.wait_ge(tables_in, 16)
                    v.memset(log_f[:], 0.0)
                    z, az = forget[:, 0], forget[:, 1]
                    then(v.tensor_tensor(z, z, forget_bias[:, layer].unsqueeze(1).broadcast_to([P, NB, HEADS]), ALU.add))
                    v.scalar_tensor_tensor(az, z, -1.0, z, ALU.mult, ALU.max).then_inc(logits_abs, 1)
                elif what == "latent_norm":
                    dve.wait_ge(log_terms, layer + 1)
                    v.scalar_tensor_tensor(log_f[:, :, 0:HEADS], forget[:, 0], 0.0, forget[:, 3], ALU.min,
                                           ALU.subtract).then_inc(forget_ready, 1)
                    scales(2 * NB)
                    for b in range(NB):
                        v.tensor_scalar(cq[:, b], cq[:, b], stat[:, 24 + b:25 + b], None, ALU.mult)
                    for b in range(NB):
                        i = v.tensor_scalar(ckvkr[:, b, 0:KV_RANK], ckvkr[:, b, 0:KV_RANK],
                                            stat[:, 26 + b:27 + b], None, ALU.mult)
                    i.then_inc(source_ready, 1)
                elif what == "cumulate":
                    if layer == 0:
                        dve.wait_ge(router_hi_ready, 1)
                        v.tensor_tensor(router_w[:, :, 1], router_raw[:], router_w.bitcast(F32)[:, :, 0],
                                        ALU.subtract).then_inc(router_lo_ready, 1)
                    dve.wait_ge(right_act, use_of_7(layer, "cumulate", 0) + 1)
                    v.tensor_tensor(cum_lo[:], ps[:, 7, 0:SEQ], cum_hi.bitcast(F32)[:], ALU.subtract)
                    v.tensor_tensor(neg_lo[:], cum_hi.bitcast(F32)[:], ps[:, 7, 0:SEQ], ALU.subtract).then_inc(neg_cum_ready, 1)
                elif what == "mla_rope_q":
                    tile_act_done(layer, "uq1")
                    dve.wait_ge(tile_dve, TILES.dve[layer, "uq1"])
                    rope(mq[:, :, :, NOPE:], ROPE // 2, const("mla_cos"), const("mla_sin")).then_inc(source_ready, 1)
                elif what == "mla_make_k":
                    tile_act_done(layer, "uk")
                    kr = ckvkr[:, :, KV_RANK:].unsqueeze(2)
                    then(rope(kr, ROPE // 2, const("mla_cos"), const("mla_sin")))
                    v.tensor_copy(mk[:, :, :, NOPE:], kr.broadcast_to([P, NB, HEADS, ROPE])).then_inc(source_ready, 1)
                elif what in ("ret_rope_q", "ret_rope_k"):
                    t = rq if what[-1] == "q" else rk
                    tile_act_done(layer, "r" + what[-1])
                    dve.wait_ge(tile_dve, TILES.dve[layer, "r" + what[-1]])
                    rope(t[:], RET_K // 2, const("ret_cos"), const("ret_sin")).then_inc(source_ready, 1)
                elif what == "softmax":
                    if k < 16:
                        n = 16 * layer + k
                        use = use_of_6(layer, "softmax", k)
                        dve.wait_ge(scores_ready, use + 1)
                        scale = 1.0 if k < HEADS else QK ** -0.5
                        mx = 30 + 2 * (k % 2)
                        for b in range(NB):
                            cols = slice(P * b, P * b + P * (b + 1))
                            i = v.tensor_tensor_reduce(
                                out=prob[:, k % 2, cols], in0=ps[:, 6, cols], in1=causal[:, P * (1 - b):],
                                scale=scale, scalar=-3e38, op0=ALU.add, op1=ALU.max, accum_out=stat[:, mx + b:mx + b + 1])
                        i.then_inc(scores_taken, 1)
                        dve.wait_ge(scores_taken, use + 1)
                        at_neg = 34 + 2 * (k % 2)
                        v.tensor_scalar(stat[:, at_neg:at_neg + 2], stat[:, mx:mx + 2], -1.0, None,
                                        ALU.mult).then_inc(row_max_ready, 1)
                    if k < 16:
                        dve.wait_ge(prob_exp, 16 * layer + k + 1)
                        sums = 38 + 2 * (k % 2)
                        inv = 46 + 2 * (k % 2)
                        then(v.reciprocal(stat[:, inv:inv + 2], stat[:, sums:sums + 2]))
                        for b in range(NB):
                            cols = slice(P * b, P * b + P * (b + 1))
                            i = v.tensor_scalar(prob[:, k % 2, cols], prob[:, k % 2, cols],
                                                stat[:, inv + b:inv + b + 1], None, ALU.mult)
                        i.then_inc(prob_ready, 1)
                    if k >= 2 and (k - 2) % 4 == 3:
                        heads_split(layer, (k - 2) // 4)
                elif what == "retention":
                    if k < HEADS:
                        use = use_of_6(layer, "retention", k)
                        dve.wait_ge(scores_ready, use + 1)
                        v.tensor_tensor(prob_T[:, k % 2, 0:SEQ], ps[:, 6, 0:SEQ], decay[:, k], ALU.mult)
                        i = v.tensor_tensor(prob_T[:, k % 2, SEQ:], ps[:, 6, SEQ:SEQ + P], decay[:, k, 0:P], ALU.mult)
                        i.then_inc(scores_taken, 1)
                    if k:
                        r = k - 1
                        dve.wait_ge(right_act, use_of_7(layer, "retention", r) + 1)
                        for b in range(NB):
                            i = v.bn_stats(bn[:, r, b], o_ret[:, b, RET_V * r:RET_V * k])
                        then(i)
                        for b in range(NB):
                            i = v.bn_aggr(ret_stat[:, b, r], bn[:, r, b])
                        i.then_inc(ret_var_ready, 1)
                elif what == "ret_norm":
                    dve.wait_ge(ret_dev_ready, layer + 1)
                    then(v.reciprocal(ret_dev[:], ret_dev[:]))
                    for b in range(NB):
                        for r in range(HEADS):
                            cols = slice(RET_V * r, RET_V * (r + 1))
                            i = v.tensor_scalar(o_ret[:, b, cols], o_ret[:, b, cols], ret_stat[:, b, r, 0:1],
                                                ret_dev[:, b, r:r + 1], ALU.subtract, ALU.mult)
                    then(i)
                    tile_act_done(layer, "rg1")
                    v.tensor_tensor(o_ret[:], o_ret[:], rg[:], ALU.mult).then_inc(source_ready, 1)

            def start():
                dve.wait_ge(params_ready, 1)
                split(0)

            def mixer(layer):
                g = G_MIX[layer]
                for step in PLAN:
                    if layer == 0 and step == ("turn", "norm0"):
                        start()
                    if step[0] == "granule":
                        split(g + AHEAD)
                        if step[3]:
                            take(layer, step[1], g)
                        g += 1
                    elif step[0] == "turn":
                        turned_tile(layer, step[1])
                        if layer == 0 and step[1] == "norm1":
                            split(1)
                    else:
                        side(layer, *step[1:])

            v.memset(eps_col[:], EPS)
            v.memset(stat[:], 0.0)
            v.memset(zeros.bitcast(F32)[:], 0.0).then_inc(zeroed, 1)
            dve.wait_ge(zeroed, 1)
            mixer(0)

            dve.sem_inc(d_act_ready, 2)
            with dve.Fori(0, N_DENSE_TURNS) as turn_no:
                def multiply(i):
                    dve.wait_ge(granule_used, turn_no * DENSE_STEP + (G_DENSE + 2 * i + 2))
                    dve.wait_ge(d_silu_ready, turn_no * 2 + (i + 1))
                    v.tensor_tensor(d_act[:, i], d_silu[:, i], ps[:, 2 * i + 1, :], ALU.mult).then_inc(d_act_ready, 1)

                def lo_part(i):
                    dve.wait_ge(d_hi_ready, turn_no * 2 + (i + 1))
                    v.tensor_tensor(d_act_lo[:, i], d_act[:, i], d_act_hi.bitcast(F32)[:, i], ALU.subtract).then_inc(d_lo_ready, 1)

                for p in range(DENSE_STEP):
                    split(G_DENSE + p + AHEAD, turn_no, 1, DENSE_STEP)
                    if p == 1:
                        multiply(0)
                    if p == 2:
                        lo_part(0)
                    if p == 3:
                        multiply(1)
                    if p == 4:
                        lo_part(1)
            dve.wait_ge(d_summed, 1)
            v.tensor_tensor(x_sb[:].rearrange("p b (n c) -> p (b n) c", n=2),
                            x_sb[:].rearrange("p b (n c) -> p (b n) c", n=2), ps[:, 4:8, :], ALU.add).then_inc(x_summed, 1)
            dve.wait_ge(x_summed, 1)
            mixer(1)

            dve.wait_ge(h_hi_ready, 1)
            v.tensor_tensor(h_lo[:], normed[:], h_hi.bitcast(F32)[:], ALU.subtract).then_inc(h_lo_ready, 1)

            logits = rt[:, LOGITS]
            dve.wait_ge(logits_turned, 1)
            parts = ps[:, 7, 0:2 * NB * N_EXPERTS].rearrange("p (b a e) -> p b a e", b=NB, a=2)
            then(v.tensor_copy(logits, parts[:, :, 0]))
            then(v.tensor_tensor(logits, logits, parts[:, :, 1], ALU.add))
            then(v.tensor_reduce(stat[:, 42:44], logits, AX.X, ALU.max))
            v.tensor_scalar(stat[:, 44:46], stat[:, 42:44], -1.0, None, ALU.mult).then_inc(logit_max_ready, 1)
            full = [P, NB, N_EXPERTS, N_EXPERTS]
            other = logits.unsqueeze(2).broadcast_to(full)
            this = logits.unsqueeze(3).broadcast_to(full)
            before = const("before").rearrange("p (i j) -> p i j", i=N_EXPERTS)
            v.tensor_tensor(pairs[:, 0], other, this, ALU.is_gt)
            then(v.tensor_tensor(pairs[:, 1], other, this, ALU.is_equal))
            then(v.tensor_tensor(pairs[:, 1], pairs[:, 1], before.unsqueeze(1).broadcast_to(full), ALU.mult))
            then(v.tensor_tensor(pairs[:, 0], pairs[:, 0], pairs[:, 1], ALU.add))
            then(v.tensor_reduce(rt[:, BEATEN], pairs[:, 0], AX.X, ALU.add))
            v.tensor_scalar(chosen_01[:], rt[:, BEATEN], 1.5, None, ALU.is_lt).then_inc(chosen_ready, 1)
            dve.wait_ge(chosen_ready, 1)
            dve.wait_ge(logit_exp, 1)
            then(v.tensor_tensor(rt[:, WEIGHTS], rt[:, EXPS], chosen_01.bitcast(F32)[:], ALU.mult))
            then(v.tensor_reduce(stat[:, 52:54], rt[:, WEIGHTS], AX.X, ALU.add))
            then(v.reciprocal(stat[:, 54:56], stat[:, 52:54]))
            then(v.tensor_tensor(rt[:, WEIGHTS], rt[:, WEIGHTS],
                                 stat[:, 54:56].unsqueeze(2).broadcast_to([P, NB, N_EXPERTS]), ALU.mult))
            v.memset(onehot_T.bitcast(F32)[:], 0.0)
            v.memset(route[:], -1.0)
            dve.wait_ge(ranks_ready, 1)
            then(v.tensor_tensor(rt[:, RANKS], chosen_01.bitcast(F32)[:],
                                 ps[:, 6, 0:NB * N_EXPERTS].rearrange("p (b e) -> p b e", b=NB), ALU.mult))
            for half in range(2):
                dst = route[:, N_EXPERTS * half:N_EXPERTS * (half + 1)]
                v.tensor_copy(dst[:, :, 2:4], rt[:, WEIGHTS].rearrange("p b e -> p e b"))
                i = v.tensor_scalar(dst[:, :, 0:2], rt[:, RANKS].rearrange("p b e -> p e b"), -1.0 - P * half, None, ALU.add)
            then(i)

            def make_onehot(E):
                v.tensor_copy(ranks_next[:].unsqueeze(1), route[:, bass.ds(E, 1), 0:2]).then_inc(ranks_copied, 1)
                dve.wait_ge(ranks_copied, E + 1)
                for b in range(NB):
                    i = v.tensor_scalar(onehot[:, b], iota, ranks_next[:, b:b + 1], None, ALU.is_equal)
                i.then_inc(onehot_ready, 1)

            ffn_weights = channel_weights("ffn", 1, KC)

            def gathered_part(E, part):
                dve.wait_ge(xg_hi_ready, E * 2 + (part + 1))
                for k in range(4 * part, 4 * part + 4):
                    i = v.scalar_tensor_tensor(xg_lo[:, k], ps[:, 2 + part, P * (k % 4):P * (k % 4 + 1)],
                                               ffn_weights[k], xg_hi.bitcast(F32)[:, k], ALU.mult, ALU.subtract)
                i.then_inc(xg_lo_ready, 1)

            def result_part(E, half):
                dve.wait_ge(y_hi_ready, E + (1 + half))
                v.tensor_tensor(y_lo[:].rearrange("p (a c) -> p a c", a=2), ps[:, 4:6, :],
                                y_hi.bitcast(F32)[:].rearrange("p (a c) -> p a c", a=2),
                                ALU.subtract).then_inc(y_lo_ready, 1)

            def add_result(E, half):
                dve.wait_ge(weights_copied, E + (half + 1))
                for u in range(N_PARTS):
                    b, cols = u // 2, slice(512 * (u % 2), 512 * (u % 2 + 1))
                    dve.wait_ge(misc_ready, E * MISC_USES + (N_PARTS * half + 1 + u))
                    v.scalar_tensor_tensor(x_sb[:, b, cols], ps[:, 6 + u % 2, :], weights_here[:, b:b + 1],
                                           x_sb[:, b, cols], ALU.mult, ALU.add).then_inc(misc_dve, 1)

            def expert(E, half):
                uses = E * MISC_USES + (N_PARTS * half + 1)

                def turned_lo(i):
                    u = N_PARTS + 1 + i
                    dve.wait_ge(misc_act, misc_taken(u, E, half)[0])
                    v.tensor_tensor(e_actT_lo[:, i % 2].rearrange("p a b -> p (a b)"), ps[:, 6 + u % 2, :],
                                    e_actT_hi.bitcast(F32)[:, i % 2].rearrange("p a b -> p (a b)"),
                                    ALU.subtract).then_inc(misc_dve, 1)

                for p, (what, i, part) in enumerate(EXPERT_ORDER):
                    split(G_MOE + p + AHEAD, E, EXPERT_G // EXPERT_RING, EXPERT_G)
                    if p == 0:
                        result_part(E, half)
                    if what == "gate" and part == 1 and i == 0:
                        add_result(E, half)
                        dve.wait_ge(misc_dve, misc_taken(N_PARTS - 1, E, half)[1])
                        v.tensor_copy(weights_here[:].unsqueeze(1), route[:, bass.ds(E, 1), 2:4]).then_inc(weights_copied, 1)
                    if what == "gate" and part == 1 and i >= 1:
                        turned_lo(i - 1)
                    if what == "up" and part == 1:
                        dve.wait_ge(granule_used, E * EXPERT_G + (G_MOE + p + 1))
                        dve.wait_ge(e_silu_ready, E * N_FT + (i + 1))
                        v.tensor_tensor(e_act[:, i % 2], e_silu[:, i % 2], ps[:, 2 * (i % 2) + 1, :],
                                        ALU.mult).then_inc(e_act_ready, 1)
                    if what == "down" and part == 1 and i == 0:
                        dve.wait_ge(misc_ready, uses + N_PARTS)
                        make_onehot(E + 1)
                    if what == "down" and part == 1 and i == N_FT - 2:
                        turned_lo(N_FT - 1)
                        gathered_part(E + 1, 1)
                    if what == "down" and part == 0 and i == N_FT - 2:
                        gathered_part(E + 1, 0)

            def expert_pass(half):
                v.memset(weights_here[:], 0.0).then_inc(weights_copied, 1)
                with dve.Fori(0, N_EXPERTS) as e:
                    expert(e + N_EXPERTS * half if half else e, half)
                result_part(N_EXPERTS * (half + 1), half)
                add_result(N_EXPERTS * (half + 1), half)
                dve.wait_ge(misc_dve, misc_taken(N_PARTS - 1, N_EXPERTS * (half + 1), half)[1])

            dve.sem_inc(misc_dve, 1)
            make_onehot(0)
            dve.wait_ge(counts_ready, 1)
            then(v.tensor_reduce(stat[:, 56:57], ps[:, 7, 0:N_EXPERTS], AX.X, ALU.max))
            v.tensor_copy(most[:], stat[:, 56:57]).then_inc(route_ready, 1)
            gathered_part(0, 0)
            gathered_part(0, 1)
            expert_pass(0)
            many = dve.value_load(most[0:1, 0:1], min_val=0, max_val=SEQ)
            with dve.If(many > P):
                expert_pass(1)
            dve.sem_inc(final_in, 1)
            dve.wait_ge(final_row_in, 16)
            for b in range(NB):
                i = v.tensor_tensor(result[:, b], x_sb[:, b], final_row[:], ALU.mult)
            then(i)
            norms[0] += 1
            dve.wait_ge(deviation, norms[0])
            v.reciprocal(stat[:, 24:24 + NB], stat[:, 16:16 + NB]).then_inc(inverse_ready, 1)
            dve.wait_ge(inverse_ready, NORMS + 1)
            v.tensor_scalar(result[:, 1], result[:, 1], stat[:, 25:26], None, ALU.mult).then_inc(final_done[1], 1)


_INS = ["x", "norm_mix_w", "w_in", "fox_f_bias", "ret_gn_w", "mla_q_norm_w", "mla_kv_norm_w", "mla_w_uq",
        "mla_w_uk", "mla_w_uv", "w_br_fox", "w_br_ret", "w_br_mla", "w_out", "norm_ffn_w", "dense_w_gate",
        "dense_w_up", "dense_w_down", "moe_w_router", "moe_w_gate", "moe_w_up", "moe_w_down", "final_norm_w"]


def kernel(**inputs):
    import numpy as _np
    import concourse.bacc as _bacc
    from concourse import mybir as _mybir
    from concourse.bass_utils import run_bass_kernel_spmd as _run

    nc = _bacc.Bacc("TRN2", target_bir_lowering=False, num_devices=1)
    arrays, args = {}, []
    for name in _INS:
        a = _np.ascontiguousarray(inputs[name])
        arrays[f"in_{name}_dram"] = a
        args.append(nc.dram_tensor(f"in_{name}_dram", a.shape, _mybir.dt.from_np(a.dtype), kind="ExternalInput").ap())
    table = shape_constants()
    arrays["in_consts_dram"] = table
    args.append(nc.dram_tensor("in_consts_dram", table.shape, _mybir.dt.float32, kind="ExternalInput").ap())
    out = nc.dram_tensor("out_0_dram", (1, SEQ, D), _mybir.dt.float32, kind="ExternalOutput").ap()
    build(nc, *args, out)
    r = _run(nc, [arrays], core_ids=[0])
    return r.results[0]["out_0_dram"]
```
